# Optimizing a Trainium2 kernel written in Bass

```python
import jax, jax.numpy as jnp
from jax import lax
import numpy as np
import math

D_MODEL = 1024
BATCH = 1
SEQ = 512
DEPTH = 1

HEAD_DIM = 64
ATTN_PAIRS = ((128, 1), (512, 4), (2048, 16))
ATTN_GROUPS = 3
ATTN_HEADS_PER_GROUP = 8
ATTN_BLOCK = 64
ROPE_THETA = 10000.0
RET_HEADS = 8
RET_QK_DIM = 64
RET_V_DIM = 128
RET_CHUNK = 128
MOE_GROUPS = 8
MOE_EXPERTS_PER_GROUP = 8
MOE_N_EXPERTS = MOE_GROUPS * MOE_EXPERTS_PER_GROUP
MOE_TOP_K = 2
MOE_HIDDEN = 512
MOE_BLOCK = 128
NORM_EPS = 1e-6

ATTN_W = ATTN_GROUPS * ATTN_HEADS_PER_GROUP * HEAD_DIM
ATTN_OUT_W = ATTN_HEADS_PER_GROUP * HEAD_DIM
RET_QK_W = RET_HEADS * RET_QK_DIM
RET_V_W = RET_HEADS * RET_V_DIM
IN_SPLIT_POINTS = (ATTN_W, 2 * ATTN_W, 3 * ATTN_W,
                   3 * ATTN_W + RET_QK_W, 3 * ATTN_W + 2 * RET_QK_W,
                   3 * ATTN_W + 2 * RET_QK_W + RET_V_W,
                   3 * ATTN_W + 2 * RET_QK_W + 2 * RET_V_W)
IN_W = IN_SPLIT_POINTS[-1] + 2 * D_MODEL


def rms_norm(x, w):
    xf = x.astype(jnp.float32)
    y = xf * lax.rsqrt(jnp.mean(xf * xf, axis=-1, keepdims=True) + NORM_EPS)
    return (y * w.astype(jnp.float32)).astype(x.dtype)

def rotary_tables(seq_len):
    inv_freq = 1.0 / (ROPE_THETA ** (jnp.arange(0, HEAD_DIM, 2, dtype=jnp.float32) / HEAD_DIM))
    ang = jnp.arange(seq_len, dtype=jnp.float32)[:, None] * inv_freq[None, :]
    return jnp.cos(ang), jnp.sin(ang)

def apply_rotary(t, cos, sin):
    t1, t2 = jnp.split(t.astype(jnp.float32), 2, axis=-1)
    c = cos[None, :, None, :]
    s = sin[None, :, None, :]
    return jnp.concatenate([t1 * c - t2 * s, t1 * s + t2 * c], axis=-1)

def dilated_window_attention(q, k, v, dilation, half):
    B, S, H, Dh = q.shape
    L = S // dilation
    nb = -(-L // ATTN_BLOCK)
    Lp = nb * ATTN_BLOCK
    N = B * dilation

    def strided(t):
        t = t.reshape(B, L, dilation, H, Dh).transpose(0, 2, 3, 1, 4)
        return t.reshape(N, H, L, Dh)

    qb = jnp.pad(strided(q), ((0, 0), (0, 0), (0, Lp - L), (0, 0))).reshape(N, H, nb, ATTN_BLOCK, Dh)

    def band(t):
        tp = jnp.pad(strided(t), ((0, 0), (0, 0), (ATTN_BLOCK, Lp - L + ATTN_BLOCK), (0, 0)))
        tb = tp.reshape(N, H, nb + 2, ATTN_BLOCK, Dh)
        return jnp.concatenate([tb[:, :, :-2], tb[:, :, 1:-1], tb[:, :, 2:]], axis=3)

    kw = band(k)
    vw = band(v)
    scores = jnp.einsum('nhbqd,nhbkd->nhbqk', qb, kw) * (Dh ** -0.5)
    blk = jnp.arange(nb)[:, None] * ATTN_BLOCK
    q_pos = blk + jnp.arange(ATTN_BLOCK)[None, :]
    k_pos = blk - ATTN_BLOCK + jnp.arange(3 * ATTN_BLOCK)[None, :]
    rel = k_pos[:, None, :] - q_pos[:, :, None]
    in_range = (k_pos[:, None, :] >= 0) & (k_pos[:, None, :] < L)
    valid = (jnp.abs(rel) <= half) & (in_range | (rel == 0))
    scores = jnp.where(valid[None, None], scores, -jnp.inf)
    m = jnp.max(scores, axis=-1, keepdims=True)
    p = jnp.exp(scores - m)
    denom = jnp.sum(p, axis=-1, keepdims=True)
    out = jnp.einsum('nhbqk,nhbkd->nhbqd', p, vw) / denom
    lse = (m + jnp.log(denom))[..., 0]
    out = out.reshape(N, H, Lp, Dh)[:, :, :L].reshape(B, dilation, H, L, Dh)
    out = out.transpose(0, 3, 1, 2, 4).reshape(B, S, H, Dh)
    lse = lse.reshape(N, H, Lp)[:, :, :L].reshape(B, dilation, H, L)
    lse = lse.transpose(0, 3, 1, 2).reshape(B, S, H)
    return out, lse

def retention_chunkwise(q, k, v, log_g):
    B, H, S, Dk = q.shape
    Dv = v.shape[-1]
    C = RET_CHUNK
    nc = S // C
    qc = q.reshape(B, H, nc, C, Dk)
    kc = k.reshape(B, H, nc, C, Dk)
    vc = v.reshape(B, H, nc, C, Dv)
    idx = jnp.arange(C, dtype=jnp.float32)
    rel = idx[:, None] - idx[None, :]
    decay = jnp.where(rel[None] >= 0, jnp.exp(jnp.maximum(rel[None], 0.0) * log_g[:, None, None]), 0.0)
    scores = jnp.einsum('bhnqd,bhnkd->bhnqk', qc, kc) * decay[None, :, None]
    inner = jnp.einsum('bhnqk,bhnkv->bhnqv', scores, vc)
    zeta = jnp.exp((C - 1 - idx)[None, :] * log_g[:, None])
    kv = jnp.einsum('bhnkd,bhnkv->nbhdv', kc * zeta[None, :, None, :, None], vc)
    chunk_decay = jnp.exp(C * log_g)[None, :, None, None]

    def step(state, kv_chunk):
        return chunk_decay * state + kv_chunk, state

    _, prev_states = lax.scan(step, jnp.zeros((B, H, Dk, Dv), jnp.float32), kv)
    xi = jnp.exp((idx + 1.0)[None, :] * log_g[:, None])
    cross = jnp.einsum('bhnqd,nbhdv->bhnqv', qc * xi[None, :, None, :, None], prev_states)
    return (inner + cross).reshape(B, H, S, Dv)

def hybrid_mixer(xn, w_in, b_branch_gate, ret_decay_fwd, ret_decay_bwd, ret_gn_w,
                 w_attn_branch, w_ret_branch, w_out, cos, sin):
    B, S, _ = xn.shape
    proj = jnp.einsum('bsd,de->bse', xn, w_in)
    q_a, k_a, v_a, q_r, k_r, v_r, g_r, gate_logits = jnp.split(proj, IN_SPLIT_POINTS, axis=-1)

    n_a = ATTN_GROUPS * ATTN_HEADS_PER_GROUP
    q_a = apply_rotary(q_a.reshape(B, S, n_a, HEAD_DIM), cos, sin).reshape(B, S, ATTN_GROUPS, ATTN_HEADS_PER_GROUP, HEAD_DIM)
    k_a = apply_rotary(k_a.reshape(B, S, n_a, HEAD_DIM), cos, sin).reshape(B, S, ATTN_GROUPS, ATTN_HEADS_PER_GROUP, HEAD_DIM)
    v_a = v_a.astype(jnp.float32).reshape(B, S, ATTN_GROUPS, ATTN_HEADS_PER_GROUP, HEAD_DIM)
    outs = []
    lses = []
    for g, (window, dilation) in enumerate(ATTN_PAIRS):
        o, l = dilated_window_attention(q_a[:, :, g], k_a[:, :, g], v_a[:, :, g], dilation, window // (2 * dilation))
        outs.append(o)
        lses.append(l)
    mix_w = jax.nn.softmax(jnp.stack(lses, axis=0), axis=0)
    y_att = jnp.einsum('gbsh,gbshd->bshd', mix_w, jnp.stack(outs, axis=0)).reshape(B, S, ATTN_OUT_W)

    q_r = apply_rotary(q_r.reshape(B, S, RET_HEADS, RET_QK_DIM), cos, sin).transpose(0, 2, 1, 3)
    k_r = (apply_rotary(k_r.reshape(B, S, RET_HEADS, RET_QK_DIM), cos, sin) * (RET_QK_DIM ** -0.5)).transpose(0, 2, 1, 3)
    v_r = v_r.astype(jnp.float32).reshape(B, S, RET_HEADS, RET_V_DIM).transpose(0, 2, 1, 3)
    log_g_fwd = jax.nn.log_sigmoid(ret_decay_fwd.astype(jnp.float32))
    log_g_bwd = jax.nn.log_sigmoid(ret_decay_bwd.astype(jnp.float32))
    ret_f = retention_chunkwise(q_r, k_r, v_r, log_g_fwd)
    ret_b = jnp.flip(retention_chunkwise(jnp.flip(q_r, 2), jnp.flip(k_r, 2), jnp.flip(v_r, 2), log_g_bwd), 2)
    ret = ret_f + ret_b
    mu = jnp.mean(ret, axis=-1, keepdims=True)
    var = jnp.mean(jnp.square(ret - mu), axis=-1, keepdims=True)
    ret = (ret - mu) * lax.rsqrt(var + NORM_EPS)
    ret = ret.transpose(0, 2, 1, 3).reshape(B, S, RET_V_W) * ret_gn_w.astype(jnp.float32)
    y_ret = jax.nn.silu(g_r.astype(jnp.float32)) * ret

    gates = jax.nn.sigmoid((gate_logits + b_branch_gate).astype(jnp.float32))
    g_att, g_ret = jnp.split(gates, 2, axis=-1)
    merged = (g_att * jnp.einsum('bse,ed->bsd', y_att, w_attn_branch.astype(jnp.float32))
              + g_ret * jnp.einsum('bse,ed->bsd', y_ret, w_ret_branch.astype(jnp.float32)))
    return jnp.einsum('bsd,de->bse', merged.astype(xn.dtype), w_out)

def hierarchical_moe(x2, w_group, b_group, w_expert, b_expert, w1, w3, w2):
    T, D = x2.shape
    xf = x2.astype(jnp.float32)
    group_p = jax.nn.softmax(xf @ w_group.astype(jnp.float32) + b_group.astype(jnp.float32), axis=-1)
    g_w, g_idx = lax.top_k(group_p, 1)
    exp_logits = (xf @ w_expert.astype(jnp.float32) + b_expert.astype(jnp.float32)).reshape(T, MOE_GROUPS, MOE_EXPERTS_PER_GROUP)
    sel_logits = jnp.take_along_axis(exp_logits, g_idx[:, :, None], axis=1)[:, 0]
    e_w, e_idx = lax.top_k(jax.nn.softmax(sel_logits, axis=-1), MOE_TOP_K)
    e_w = e_w / jnp.sum(e_w, axis=-1, keepdims=True)
    gate = (g_w * e_w).reshape(-1)
    eid = (g_idx * MOE_EXPERTS_PER_GROUP + e_idx).reshape(-1).astype(jnp.int32)
    tok = jnp.repeat(jnp.arange(T, dtype=jnp.int32), MOE_TOP_K)
    A = T * MOE_TOP_K

    order = jnp.argsort(eid)
    s_eid = eid[order]
    s_tok = tok[order]
    s_gate = gate[order]
    counts = jnp.bincount(eid, length=MOE_N_EXPERTS)
    starts = jnp.cumsum(counts) - counts
    padded = (counts + MOE_BLOCK - 1) // MOE_BLOCK * MOE_BLOCK
    p_ends = jnp.cumsum(padded)
    p_starts = p_ends - padded
    dest = p_starts[s_eid] + (jnp.arange(A, dtype=jnp.int32) - starts[s_eid])
    n_blocks = -(-A // MOE_BLOCK) + MOE_N_EXPERTS
    slot_tok = jnp.full((n_blocks * MOE_BLOCK,), T, jnp.int32).at[dest].set(s_tok)
    blk_eid = jnp.clip(jnp.searchsorted(p_ends, jnp.arange(n_blocks) * MOE_BLOCK, side='right'), 0, MOE_N_EXPERTS - 1)
    x_pad = jnp.concatenate([x2, jnp.zeros((1, D), x2.dtype)], axis=0)
    x_slots = x_pad[slot_tok].reshape(n_blocks, MOE_BLOCK, D)

    def expert_block(args):
        xb, e = args
        hid = jax.nn.silu(xb @ w1[e]) * (xb @ w3[e])
        return hid @ w2[e]

    y_slots = lax.map(expert_block, (x_slots, blk_eid)).reshape(n_blocks * MOE_BLOCK, D)
    y_assign = y_slots[dest].astype(jnp.float32) * s_gate[:, None]
    return jax.ops.segment_sum(y_assign, s_tok, num_segments=T).astype(x2.dtype)

def first_inputs(seed: int = 0) -> dict:
    key = jax.random.key(seed)
    ks = jax.random.split(key, 20)
    L = DEPTH
    f32 = jnp.float32

    def nrm(k, shape, scale):
        return jax.random.normal(k, shape, f32) * scale

    heads = jnp.arange(RET_HEADS, dtype=f32)
    decay_logit = jnp.log(2.0 ** (5.0 + heads) - 1.0)
    return {
        'x': nrm(ks[0], (BATCH, SEQ, D_MODEL), 1.0),
        'norm_mix_w': 1.0 + nrm(ks[1], (L, D_MODEL), 0.02),
        'w_in': nrm(ks[2], (L, D_MODEL, IN_W), D_MODEL ** -0.5),
        'b_branch_gate': nrm(ks[3], (L, 2 * D_MODEL), 0.02),
        'ret_decay_fwd': decay_logit[None] + nrm(ks[4], (L, RET_HEADS), 0.05),
        'ret_decay_bwd': decay_logit[None] + nrm(ks[5], (L, RET_HEADS), 0.05),
        'ret_gn_w': 1.0 + nrm(ks[6], (L, RET_V_W), 0.02),
        'w_attn_branch': nrm(ks[7], (L, ATTN_OUT_W, D_MODEL), ATTN_OUT_W ** -0.5),
        'w_ret_branch': nrm(ks[8], (L, RET_V_W, D_MODEL), RET_V_W ** -0.5),
        'w_out': nrm(ks[9], (L, D_MODEL, D_MODEL), D_MODEL ** -0.5),
        'norm_moe_w': 1.0 + nrm(ks[10], (L, D_MODEL), 0.02),
        'moe_w_group': nrm(ks[11], (L, D_MODEL, MOE_GROUPS), D_MODEL ** -0.5),
        'moe_b_group': nrm(ks[12], (L, MOE_GROUPS), 0.01),
        'moe_w_expert': nrm(ks[13], (L, D_MODEL, MOE_N_EXPERTS), D_MODEL ** -0.5),
        'moe_b_expert': nrm(ks[14], (L, MOE_N_EXPERTS), 0.01),
        'moe_w1': nrm(ks[15], (L, MOE_N_EXPERTS, D_MODEL, MOE_HIDDEN), D_MODEL ** -0.5),
        'moe_w3': nrm(ks[16], (L, MOE_N_EXPERTS, D_MODEL, MOE_HIDDEN), D_MODEL ** -0.5),
        'moe_w2': nrm(ks[17], (L, MOE_N_EXPERTS, MOE_HIDDEN, D_MODEL), MOE_HIDDEN ** -0.5),
        'norm_final_w': 1.0 + nrm(ks[18], (D_MODEL,), 0.02),
    }

def first_block(x, norm_mix_w, w_in, b_branch_gate, ret_decay_fwd, ret_decay_bwd, ret_gn_w,
              w_attn_branch, w_ret_branch, w_out, norm_moe_w, moe_w_group, moe_b_group,
              moe_w_expert, moe_b_expert, moe_w1, moe_w3, moe_w2, norm_final_w):
    B, S, D = x.shape
    cos, sin = rotary_tables(S)
    h = x
    for l in range(DEPTH):
        xn = rms_norm(h, norm_mix_w[l])
        mix = hybrid_mixer(xn, w_in[l], b_branch_gate[l], ret_decay_fwd[l], ret_decay_bwd[l], ret_gn_w[l],
                           w_attn_branch[l], w_ret_branch[l], w_out[l], cos, sin)
        h = h + mix.astype(h.dtype)
        hn = rms_norm(h, norm_moe_w[l])
        ffn = hierarchical_moe(hn.reshape(B * S, D), moe_w_group[l], moe_b_group[l], moe_w_expert[l],
                               moe_b_expert[l], moe_w1[l], moe_w3[l], moe_w2[l])
        h = h + ffn.reshape(B, S, D).astype(h.dtype)
    return rms_norm(h, norm_final_w)


DEPTH_2 = 2

D_MIX = D_MODEL
MLA_HEADS = 4
MLA_NOPE = 128
MLA_ROPE = 64
MLA_V = 128
Q_LORA = 384
KV_LORA = 256
ROPE_BASE = 10000.0
Q_BLOCK = 128
MLA_W = MLA_HEADS * MLA_V
POOL_WINDOWS = (2, 4, 8, 16)
POOL_GROUPS = 4
POOL_CH = 64
POOL_W = POOL_GROUPS * POOL_CH
M_HEADS = 4
M_HEAD_DIM = 64
M_W = M_HEADS * M_HEAD_DIM
M_CONV = 4
M_CHUNK = 64
D_FF = 2816
FFN_CONV = 3
LN_EPS = 1e-5
RMS_EPS = 1e-6
ALPHA = (2 * DEPTH_2) ** 0.25
BETA = (8 * DEPTH_2) ** -0.25

IN_SIZES = (Q_LORA, KV_LORA, MLA_ROPE, POOL_W, M_W, M_W, M_W, M_HEADS, M_HEADS)
D_IN = Q_LORA + KV_LORA + MLA_ROPE + POOL_W + 3 * M_W + 2 * M_HEADS


def _split_points():
    return [int(v) for v in np.cumsum(np.array(IN_SIZES))[:-1]]

def layer_norm(x, g, b):
    xf = x.astype(jnp.float32)
    mu = jnp.mean(xf, axis=-1, keepdims=True)
    var = jnp.mean(jnp.square(xf - mu), axis=-1, keepdims=True)
    y = (xf - mu) * lax.rsqrt(var + LN_EPS) * g + b
    return y.astype(x.dtype)

def rms_norm_2(x, g):
    xf = x.astype(jnp.float32)
    y = xf * lax.rsqrt(jnp.mean(jnp.square(xf), axis=-1, keepdims=True) + RMS_EPS) * g
    return y.astype(x.dtype)

def rotary_tables_2(seq, dim):
    inv = 1.0 / (ROPE_BASE ** (jnp.arange(0, dim, 2, dtype=jnp.float32) / dim))
    ang = jnp.arange(seq, dtype=jnp.float32)[:, None] * inv[None, :]
    return jnp.cos(ang), jnp.sin(ang)

def apply_rotary_2(x, cos, sin):
    xf = x.astype(jnp.float32)
    half = xf.shape[-1] // 2
    x1, x2 = xf[..., :half], xf[..., half:]
    return jnp.concatenate([x1 * cos - x2 * sin, x2 * cos + x1 * sin], axis=-1).astype(x.dtype)

def causal_dwconv(x, w, b):
    k = w.shape[0]
    y = lax.conv_general_dilated(
        x, w[:, None, :], window_strides=(1,), padding=((k - 1, 0),),
        dimension_numbers=("NWC", "WIO", "NWC"), feature_group_count=x.shape[-1])
    return y + b

def mla(cq, ckv, kr, g_qn, w_uq, g_kvn, w_ukv, cos, sin):
    B, S, _ = cq.shape
    H = MLA_HEADS
    q = (rms_norm_2(cq, g_qn) @ w_uq).reshape(B, S, H, MLA_NOPE + MLA_ROPE)
    q_nope, q_pe = q[..., :MLA_NOPE], q[..., MLA_NOPE:]
    q_pe = apply_rotary_2(q_pe, cos[:, None, :], sin[:, None, :])
    kv = (rms_norm_2(ckv, g_kvn) @ w_ukv).reshape(B, S, H, MLA_NOPE + MLA_V)
    k_nope, v = kv[..., :MLA_NOPE], kv[..., MLA_NOPE:]
    k_pe = apply_rotary_2(kr, cos, sin)
    scale = (MLA_NOPE + MLA_ROPE) ** -0.5
    nb = S // Q_BLOCK
    qn_b = (q_nope * scale).reshape(B, nb, Q_BLOCK, H, MLA_NOPE).transpose(1, 0, 3, 2, 4)
    qp_b = (q_pe * scale).reshape(B, nb, Q_BLOCK, H, MLA_ROPE).transpose(1, 0, 3, 2, 4)
    k_nope_t = k_nope.transpose(0, 2, 1, 3)
    v_t = v.transpose(0, 2, 1, 3)
    key_pos = jnp.arange(S)

    def block(args):
        qn, qp, start = args
        s = (jnp.einsum("bhqd,bhkd->bhqk", qn, k_nope_t)
             + jnp.einsum("bhqd,bkd->bhqk", qp, k_pe)).astype(jnp.float32)
        q_pos = start + jnp.arange(Q_BLOCK)
        s = jnp.where(key_pos[None, :] <= q_pos[:, None], s, -jnp.inf)
        p = jax.nn.softmax(s, axis=-1).astype(v_t.dtype)
        return jnp.einsum("bhqk,bhkd->bhqd", p, v_t)

    o = lax.map(block, (qn_b, qp_b, jnp.arange(nb) * Q_BLOCK))
    return o.transpose(1, 0, 3, 2, 4).reshape(B, S, H * MLA_V).astype(cq.dtype)

def multiscale_pool(p, w_pool, s_pool):
    B, S, _ = p.shape
    G, C = POOL_GROUPS, POOL_CH
    pg = p.reshape(B, S, G, C).astype(jnp.float32)
    cs = jnp.concatenate([jnp.zeros((B, 1, G, C), jnp.float32), jnp.cumsum(pg, axis=1)], axis=1)
    t = jnp.arange(S)
    win = jnp.array(POOL_WINDOWS, dtype=jnp.int32)
    lo = jnp.maximum(t[:, None] + 1 - win[None, :], 0)
    window_sum = cs[:, 1:] - cs[:, lo, jnp.arange(G)[None, :]]
    count = (t[:, None] + 1 - lo).astype(jnp.float32)
    y = (window_sum / count[None, :, :, None] - pg).astype(p.dtype)
    y = jnp.einsum("bsgc,gcd->bsgd", y, w_pool) * s_pool.reshape(G, C)
    return y.reshape(B, S, G * C).astype(p.dtype)

def mlstm(xqk, xv, xo, ipre, fpre, w_mconv, b_mconv, w_mq, w_mk, b_i, b_f, g_mh):
    B, S, _ = xqk.shape
    H, Dh, L = M_HEADS, M_HEAD_DIM, M_CHUNK
    nc = S // L
    c = jax.nn.silu(causal_dwconv(xqk, w_mconv, b_mconv)).reshape(B, S, H, Dh)
    q = jnp.einsum("bshd,hde->bshe", c, w_mq).astype(jnp.float32)
    k = (jnp.einsum("bshd,hde->bshe", c, w_mk) * (Dh ** -0.5)).astype(jnp.float32)
    v = xv.reshape(B, S, H, Dh).astype(jnp.float32)
    log_i = (ipre + b_i).astype(jnp.float32)
    log_f = jax.nn.log_sigmoid((fpre + b_f).astype(jnp.float32))

    def to_chunks4(a):
        return a.reshape(B, nc, L, H, Dh).transpose(1, 0, 3, 2, 4)

    def to_chunks3(a):
        return a.reshape(B, nc, L, H).transpose(1, 0, 3, 2)

    tri = jnp.tril(jnp.ones((L, L), dtype=bool))

    def step(carry, inp):
        Cm, n, m = carry
        qc, kc, vc, li, lf = inp
        b = jnp.cumsum(lf, axis=-1)
        D = jnp.where(tri, b[..., :, None] - b[..., None, :] + li[..., None, :], -jnp.inf)
        inter = b + m[..., None]
        m_t = jnp.maximum(inter, jnp.max(D, axis=-1))
        g = jnp.exp(inter - m_t)
        sc = jnp.einsum("bhtd,bhsd->bhts", qc, kc) * jnp.exp(D - m_t[..., None])
        num = g[..., None] * jnp.einsum("bhtd,bhde->bhte", qc, Cm) + jnp.einsum("bhts,bhse->bhte", sc, vc)
        den = g * jnp.einsum("bhtd,bhd->bht", qc, n) + jnp.sum(sc, axis=-1)
        h = num / jnp.maximum(jnp.abs(den), jnp.exp(-m_t))[..., None]
        bL = b[..., -1]
        w_log = bL[..., None] - b + li
        m_new = jnp.maximum(bL + m, jnp.max(w_log, axis=-1))
        w = jnp.exp(w_log - m_new[..., None])
        decay = jnp.exp(bL + m - m_new)
        C_new = decay[..., None, None] * Cm + jnp.einsum("bhs,bhsd,bhse->bhde", w, kc, vc)
        n_new = decay[..., None] * n + jnp.einsum("bhs,bhsd->bhd", w, kc)
        return (C_new, n_new, m_new), h

    init = (jnp.zeros((B, H, Dh, Dh), jnp.float32), jnp.zeros((B, H, Dh), jnp.float32),
            jnp.zeros((B, H), jnp.float32))
    _, hs = lax.scan(step, init, (to_chunks4(q), to_chunks4(k), to_chunks4(v),
                                  to_chunks3(log_i), to_chunks3(log_f)))
    h = hs.transpose(1, 0, 3, 2, 4).reshape(B, S, H, Dh)
    mu = jnp.mean(h, axis=-1, keepdims=True)
    var = jnp.mean(jnp.square(h - mu), axis=-1, keepdims=True)
    h = (h - mu) * lax.rsqrt(var + LN_EPS) * g_mh.reshape(H, Dh)
    out = jax.nn.sigmoid(xo.astype(jnp.float32)).reshape(B, S, H, Dh) * h
    return out.reshape(B, S, M_W).astype(xqk.dtype)

def conv_glu_ffn(x, w_up, w_fconv, b_fconv, w_down):
    a, g = jnp.split(x @ w_up, 2, axis=-1)
    g = causal_dwconv(g, w_fconv, b_fconv)
    return (jax.nn.silu(g) * a) @ w_down

def second_inputs(seed: int = 0) -> dict:
    key = jax.random.key(seed)
    ks = jax.random.split(key, 32)
    f32 = jnp.float32

    def nrm(k, shape, scale):
        return jax.random.normal(k, shape, f32) * scale

    def gain(k, shape):
        return 1.0 + 0.02 * jax.random.normal(k, shape, f32)

    L = DEPTH_2
    return {
        "x": nrm(ks[0], (BATCH, SEQ, D_MODEL), 1.0),
        "ln0_g": gain(ks[1], (D_MODEL,)),
        "ln0_b": nrm(ks[2], (D_MODEL,), 0.02),
        "w_in": nrm(ks[3], (L, D_MODEL, D_IN), D_MODEL ** -0.5),
        "g_qn": gain(ks[4], (L, Q_LORA)),
        "w_uq": nrm(ks[5], (L, Q_LORA, MLA_HEADS * (MLA_NOPE + MLA_ROPE)), Q_LORA ** -0.5),
        "g_kvn": gain(ks[6], (L, KV_LORA)),
        "w_ukv": nrm(ks[7], (L, KV_LORA, MLA_HEADS * (MLA_NOPE + MLA_V)), KV_LORA ** -0.5),
        "w_pool": nrm(ks[8], (L, POOL_GROUPS, POOL_CH, POOL_CH), POOL_CH ** -0.5),
        "s_pool": gain(ks[9], (L, POOL_W)),
        "w_mconv": nrm(ks[10], (L, M_CONV, M_W), M_CONV ** -0.5),
        "b_mconv": nrm(ks[11], (L, M_W), 0.02),
        "w_mq": nrm(ks[12], (L, M_HEADS, M_HEAD_DIM, M_HEAD_DIM), M_HEAD_DIM ** -0.5),
        "w_mk": nrm(ks[13], (L, M_HEADS, M_HEAD_DIM, M_HEAD_DIM), M_HEAD_DIM ** -0.5),
        "b_i": nrm(ks[14], (L, M_HEADS), 0.1),
        "b_f": jnp.linspace(3.0, 6.0, M_HEADS, dtype=f32)[None, :] + nrm(ks[15], (L, M_HEADS), 0.1),
        "g_mh": gain(ks[16], (L, M_W)),
        "w_out": nrm(ks[17], (L, D_MIX, D_MODEL), BETA * D_MIX ** -0.5),
        "ln1_g": gain(ks[18], (L, D_MODEL)),
        "ln1_b": nrm(ks[19], (L, D_MODEL), 0.02),
        "w_up": nrm(ks[20], (L, D_MODEL, 2 * D_FF), D_MODEL ** -0.5),
        "w_fconv": nrm(ks[21], (L, FFN_CONV, D_FF), FFN_CONV ** -0.5),
        "b_fconv": nrm(ks[22], (L, D_FF), 0.02),
        "w_down": nrm(ks[23], (L, D_FF, D_MODEL), BETA * D_FF ** -0.5),
        "ln2_g": gain(ks[24], (L, D_MODEL)),
        "ln2_b": nrm(ks[25], (L, D_MODEL), 0.02),
    }

def second_block(x, ln0_g, ln0_b, w_in, g_qn, w_uq, g_kvn, w_ukv, w_pool, s_pool, w_mconv,
              b_mconv, w_mq, w_mk, b_i, b_f, g_mh, w_out, ln1_g, ln1_b, w_up, w_fconv,
              b_fconv, w_down, ln2_g, ln2_b):
    S = x.shape[1]
    cos, sin = rotary_tables_2(S, MLA_ROPE)
    h = layer_norm(x, ln0_g, ln0_b)
    for l in range(DEPTH_2):
        proj = h @ w_in[l]
        cq, ckv, kr, xp, xqk, xv, xo, ipre, fpre = jnp.split(proj, _split_points(), axis=-1)
        a = mla(cq, ckv, kr, g_qn[l], w_uq[l], g_kvn[l], w_ukv[l], cos, sin)
        p = multiscale_pool(xp, w_pool[l], s_pool[l])
        m = mlstm(xqk, xv, xo, ipre, fpre, w_mconv[l], b_mconv[l], w_mq[l], w_mk[l],
                  b_i[l], b_f[l], g_mh[l])
        mix = jnp.concatenate([a.astype(h.dtype), p.astype(h.dtype), m.astype(h.dtype)], axis=-1) @ w_out[l]
        h = layer_norm(ALPHA * h + mix, ln1_g[l], ln1_b[l])
        f = conv_glu_ffn(h, w_up[l], w_fconv[l], b_fconv[l], w_down[l])
        h = layer_norm(ALPHA * h + f, ln2_g[l], ln2_b[l])
    return h


def setup_inputs(seed=0):
    out = dict(first_inputs(seed))
    for name, value in second_inputs(seed + 1).items():
        if name != "x":
            out[name + "_2"] = value
    return out


def reference(
    x, norm_mix_w, w_in, b_branch_gate, ret_decay_fwd, ret_decay_bwd, ret_gn_w, w_attn_branch,
    w_ret_branch, w_out, norm_moe_w, moe_w_group, moe_b_group, moe_w_expert, moe_b_expert,
    moe_w1, moe_w3, moe_w2, norm_final_w, ln0_g_2, ln0_b_2, w_in_2, g_qn_2, w_uq_2, g_kvn_2,
    w_ukv_2, w_pool_2, s_pool_2, w_mconv_2, b_mconv_2, w_mq_2, w_mk_2, b_i_2, b_f_2, g_mh_2,
    w_out_2, ln1_g_2, ln1_b_2, w_up_2, w_fconv_2, b_fconv_2, w_down_2, ln2_g_2, ln2_b_2,
):
    x = first_block(
        x, norm_mix_w, w_in, b_branch_gate, ret_decay_fwd, ret_decay_bwd, ret_gn_w,
        w_attn_branch, w_ret_branch, w_out, norm_moe_w, moe_w_group, moe_b_group, moe_w_expert,
        moe_b_expert, moe_w1, moe_w3, moe_w2, norm_final_w,
    )
    return second_block(
        x, ln0_g_2, ln0_b_2, w_in_2, g_qn_2, w_uq_2, g_kvn_2, w_ukv_2, w_pool_2, s_pool_2,
        w_mconv_2, b_mconv_2, w_mq_2, w_mk_2, b_i_2, b_f_2, g_mh_2, w_out_2, ln1_g_2, ln1_b_2,
        w_up_2, w_fconv_2, b_fconv_2, w_down_2, ln2_g_2, ln2_b_2,
    )


_drawn_inputs = setup_inputs


def setup_inputs(seed=0):
    import zlib

    import numpy as np

    out = dict(_drawn_inputs(seed))
    spreads = {}
    factors = {'b_branch_gate': 5.31,
     'ret_gn_w': 2.783,
     'moe_b_group': 6.992,
     'moe_b_expert': 3.96,
     'norm_final_w': 2.682,
     'g_qn_2': 8.0,
     'g_kvn_2': 8.0,
     's_pool_2': 8.0,
     'b_mconv_2': 8.0,
     'b_i_2': 64.0,
     'g_mh_2': 8.0,
     'b_fconv_2': 8.0}
    for name, (base, spread) in spreads.items():
        noise = np.random.default_rng([zlib.crc32(name.encode()), seed]).standard_normal(out[name].shape)
        drawn = base * np.exp(spread * noise) if base else spread * noise
        out[name] = __import__('jax').numpy.asarray(drawn.astype(out[name].dtype))
    for name, factor in factors.items():
        out[name] = (out[name] * factor).astype(out[name].dtype)
    return out
```

```python
import numpy as np
import concourse.bass as bass
from concourse import mybir
from contextlib import ExitStack

f32 = mybir.dt.float32
i32 = mybir.dt.int32
ALU = mybir.AluOpType
ACT = mybir.ActivationFunctionType
AX = mybir.AxisListType

P = 128
S = 512
T = S // P
D = 1024
KT = D // P
EPS = 1e-6
NEG = -1.0e30

AG, AH, HD = 3, 8, 64
AW = AG * AH * HD
DIL = (1, 4, 16)
HALF = 64
RH, RK, RV = 8, 64, 128
WB = 2 * S - P
WOFF = S - P
CW = 384


class Tick:

    def __init__(self, eng, sem):
        self.eng, self.sem, self.n = eng, sem, 0

    def __call__(self, ins):
        ins.then_inc(self.sem, 1)
        self.n += 1
        return self.n

    def wait(self, n):
        self.eng.wait_ge(self.sem, n)


class Need:

    def __init__(self, eng):
        self.eng, self.seen = eng, {}

    def __call__(self, sem, n):
        if n > self.seen.get(sem.name, 0):
            self.eng.wait_ge(sem, n)
            self.seen[sem.name] = n


def constants():
    p = np.arange(P)[:, None]
    c = np.arange(WB)[None, :] - WOFF
    t = {}
    t["ident"] = np.eye(P)
    inv = (1.0 / (np.float32(10000.0) ** (np.arange(0, HD, 2, dtype=np.float32) / np.float32(HD)))).astype(np.float32)
    ang = (np.arange(S, dtype=np.float32)[:, None] * inv[None, :]).astype(np.float32)
    cos, sin = np.cos(ang.astype(np.float64)), np.sin(ang.astype(np.float64))
    t["cos"] = cos.reshape(T, P, HD // 2).transpose(1, 0, 2).reshape(P, -1)
    t["sin"] = sin.reshape(T, P, HD // 2).transpose(1, 0, 2).reshape(P, -1)
    t["nsin"] = -t["sin"]
    for g, d in enumerate(DIL):
        rel = c - p
        ok = (rel % d == 0) & (np.abs(rel) <= HALF * d)
        t[f"mask{g}"] = np.where(ok, 0.0, NEG)
    t["fwd"] = np.maximum(c - p, 0)
    t["bwd"] = np.maximum(p - c, 0)
    t["same"] = (c == p) * 1.0
    t["iota"] = np.broadcast_to(np.arange(P)[None, :], (P, P))
    t["before"] = (p < np.arange(P)[None, :]) * 1.0
    t["ones"] = np.ones((P, P))
    t["piota"] = p
    return {k: np.ascontiguousarray(v, dtype=np.float32) for k, v in t.items()}


def const_columns():
    at, out = 0, {}
    for k, v in constants().items():
        out[k] = (at, v.shape[1])
        at += v.shape[1]
    return out, at


STEPS = ([("A", q, g, t) for q in range(4) for g in range(AG) for t in range(T)]
         + [(k, hp, 0, t) for hp in range(4) for k in ("R1", "R2") for t in range(T)]
         + [("G", j // 2, j % 2, 0) for j in range(16)])
NPROJ = len(STEPS)


def units():
    out = {}
    for q in range(4):
        for i in range(8):
            at = 12 * (q + 1) + 2 + i
            out[at] = ("att", q, i % 2, i // 2)
    for hp in range(4):
        for k in range(2):
            out[48 + 8 * (hp + 1) + 3 + 3 * k] = ("ret", hp, k, 0)
    return out


UNITS = units()
UORDER = [UNITS[s] for s in sorted(UNITS)]
ATT_UNITS = [u for u in UORDER if u[0] == "att"]
RET_UNITS = [u for u in UORDER if u[0] == "ret"]


def att_keys(g, t):
    reach = -(-HALF * DIL[g] // P)
    return list(range(max(0, t - reach), min(T, t + reach + 1)))


def att_blocks(t):
    return [(g, k) for g in range(AG) for k in att_keys(g, t)]


def att_chunks(t):
    b = att_blocks(t)
    return [b[i:i + 4] for i in range(0, len(b), 4)]


def chunk_no(s):
    return s // 4 if s < 80 else 20 + (s - 80) // 2


N_CHUNK = 28
NSLOT = 3


def rope_steps():
    return [s for s, x in enumerate(STEPS) if x[0] in ("A", "R1")]


HP2 = 2 * HD
ARENA = 53200


def tile(t, n=P):
    return slice(t * n, (t + 1) * n)


class Space:

    def __init__(self, arena, at=0):
        self.arena, self.at = arena, at

    def __call__(self, *shape):
        n = int(np.prod(shape))
        v = self.arena[:, self.at:self.at + n]
        self.at += n
        assert self.at <= ARENA, self.at
        if len(shape) == 2:
            v = v.rearrange("p (a b) -> p a b", a=shape[0])
        if len(shape) == 3:
            v = v.rearrange("p (a b c) -> p a b c", a=shape[0], b=shape[1])
        return v


class Mem:
    pass


def persistent(arena):
    m = Mem()
    m.arena = arena
    sp = Space(arena)
    m.h = sp(T, D)
    m.aT = sp(KT, S)
    m.ident = sp(P)
    m.free = sp.at
    return m


def mixer_memory(arena):
    m = persistent(arena)
    sp = Space(arena, m.free)
    at = sp.at
    m.cos, m.sin, m.nsin = (sp(T, HD // 2) for _ in range(3))
    m.trig = Space(arena, at)(3 * T * HD // 2)
    m.tabs = sp(3, WB)
    m.decay, m.lg = sp(2, RH), sp(2, RH)
    m.ls = sp(6, 2 * RH)
    m.gnw, m.gate_b, m.half = sp(D), sp(16), sp(1)
    m.ring_at = sp.at
    m.ring = [sp(KT, CW) for _ in range(NSLOT)]
    at = sp.at
    m.ssb = [sp(11 * P) for _ in range(2)]
    m.sd = Space(arena, at)(T, S)
    m.y_att = sp(T, AH * HD)
    m.rqk_at = sp.at
    m.rqk = [sp(2, S) for _ in range(2)]
    m.rv = [sp(T, 2 * RV) for _ in range(2)]
    m.rg = [sp(T, 2 * RV) for _ in range(2)]
    m.dt_at = sp.at
    m.dt = [sp(WB) for _ in range(2)]
    m.e12 = sp(2, WB)
    m.ra = [sp(4, 2, HD // 2) for _ in range(2)]
    m.rb = [sp(4, 2, HD // 2) for _ in range(2)]
    m.rot = [sp(2 * HP2) for _ in range(2)]
    m.mx = [sp(4) for _ in range(2)]
    m.negm, m.den, m.rden = ([sp(1) for _ in range(2)] for _ in range(3))
    m.bst, m.bmv, m.rstd = sp(T, 6), sp(T, 2), sp(T)
    m.rn, m.rn2 = sp(T, RV), sp(T, RV)
    q0 = sp.at
    m.qk, m.v = [sp(AG, 2, S)], [sp(T, AG, HP2)]
    q1 = sp.at
    m.qk.append(sp(AG, 2, S))
    m.v.append(sp(T, AG, HP2))
    m.masks = sp(AG, WB)
    m.pt = sp(11 * P)
    m.y_ret = Space(arena, q0)(T, RH * RV)
    m.gates = Space(arena, q1)(16, S)
    return m


MIXER_SEMS = [
    "proj_done", "rope_read", "rot_ready", "proj_read", "t_done", "qk_ready", "s_done", "s_masked",
    "negm_ready", "exp_done", "pt_done", "pt_ready", "pv_done", "y_done", "rs_done", "sd_ready",
    "ro_done", "var_ready", "rstd_ready", "rn_ready", "ry_ready", "e_ready", "dt_ready",
    "lg_half", "lg_ready", "tables_in", "smalls_in", "mask_in",
    "dve_step", "act_step", "pool_step"] + [f"w_in{i}" for i in range(NSLOT)]


def mixer_loads():
    out = []
    for q in range(4):
        for g in range(AG):
            out.append([(i * AW + g * AH * HD + q * HP2, HP2, i * HP2) for i in range(3)])
    base = 3 * AW
    for hp in range(4):
        out.append([(base + hp * P, P, 0), (base + 512 + hp * P, P, P),
                    (base + 1024 + hp * 256, P, 2 * P)])
        out.append([(base + 1024 + hp * 256 + P, P, 0), (base + 2048 + hp * 256, 256, P)])
    for j in range(8):
        out.append([(base + 3072 + j * 256, 256, 0)])
    return out


MLOADS = mixer_loads()


def mload_count(c):
    return 16 * sum(len(MLOADS[i]) for i in range(c % NSLOT, c + 1, NSLOT))


def steps_of_chunk(c):
    return [s for s in range(NPROJ) if chunk_no(s) == c]


def sp_first(sp, A, m, G):
    w_in = A["w_in"][0].rearrange("(k p) n -> p k n", p=P)
    for c in range(NSLOT):
        for src, n, dst in MLOADS[c]:
            sp.dma_start(m.ring[c][:, :, dst:dst + n], w_in[:, :, src:src + n])\
              .then_inc(G[f"w_in{c}"], 16)


def sp_mixer(sp, A, m, G):
    need = Need(sp)
    w_in = A["w_in"][0].rearrange("(k p) n -> p k n", p=P)
    for c, parts in enumerate(MLOADS):
        if c < NSLOT:
            continue
        if c >= NSLOT:
            need(G["proj_done"], steps_of_chunk(c - NSLOT)[-1] + 1)
        for src, n, dst in parts:
            sp.dma_start(m.ring[c % NSLOT][:, :, dst:dst + n], w_in[:, :, src:src + n])\
              .then_inc(G[f"w_in{c % NSLOT}"], 16)


NSTEP = NPROJ + 2
ROPES = [s for s, x in enumerate(STEPS) if x[0] in ("A", "R1")]


def ropes_to(s):
    return sum(r <= s for r in ROPES)


def att_index(u):
    return ATT_UNITS.index(u)


def chunks_before(a):
    return sum(len(att_chunks(u[3])) for u in ATT_UNITS[:a])


def pe_mixer(nc, pe, m, G, banks):
    need = Need(pe)
    for s in range(NSTEP):
        if s < NPROJ:
            kind, a, b, t = STEPS[s]
            c = chunk_no(s)
            need(G[f"w_in{c % NSLOT}"], mload_count(c))
            need(G["proj_read"], s - 1)
            w = m.ring[c % NSLOT]
            for k in range(KT):
                if kind == "G":
                    ins = pe.matmul(banks[s % 2][:, :], w[:, k, tile(b)], m.aT[:, k, :],
                                    start=(k == 0), stop=(k == KT - 1))
                else:
                    ins = pe.matmul(banks[s % 2][:, 0:CW], m.aT[:, k, tile(t)], w[:, k, :],
                                    start=(k == 0), stop=(k == KT - 1))
            ins.then_inc(G["proj_done"], 1)
        if s - 1 in ROPES:
            n = ROPES.index(s - 1)
            need(G["rot_ready"], n + 1)
            need(G["qk_ready"], n)
            need(G["y_done"], sum(x < s - 1 for x in UNITS if UNITS[x][0] == "att"))
            for i in range(2):
                ins = pe.transpose(banks[2][:, tile(i)], m.rot[n % 2][:, tile(i)], m.ident)
            ins.then_inc(G["t_done"], 1)
        u = UNITS.get(s)
        if u and u[0] == "att":
            _, q, hh, t = u
            a, rows = att_index(u), slice(HD * hh, HD * hh + HD)
            need(G["qk_ready"], 12 * (q + 1))
            need(G["s_masked"], a)
            qk = m.qk[q % 2]
            for g in range(AG):
                ks = att_keys(g, t)
                ins = pe.matmul(banks[3 + g][:, 0:P * len(ks)], qk[rows, g, 0, tile(t)],
                                qk[rows, g, 1, ks[0] * P:(ks[-1] + 1) * P], start=True, stop=True)
            ins.then_inc(G["s_done"], 1)
        if u and u[0] == "ret":
            _, hp, k, _ = u
            r, rows = RET_UNITS.index(u), slice(RK * k, RK * k + RK)
            need(G["qk_ready"], 48 + 4 * (hp + 1))
            need(G["s_masked"], len(ATT_UNITS))
            need(G["pt_ready"], chunks_before(len(ATT_UNITS)))
            need(G["sd_ready"], 4 * r)
            for kt in range(T):
                pe.matmul(banks[3 + kt][:, :], m.rqk[hp % 2][rows, 1, tile(kt)],
                          m.rqk[hp % 2][rows, 0, :], start=True, stop=True).then_inc(G["rs_done"], 1)
        u = UNITS.get(s - 1)
        if u and u[0] == "att":
            _, q, hh, t = u
            a = att_index(u)
            need(G["exp_done"], a + 1)
            chunks, n0 = att_chunks(t), chunks_before(a)

            def turn(i):
                need(G["pt_ready"], n0 + i - 1)
                for j in range(len(chunks[i])):
                    ins = pe.transpose(banks[6 + (n0 + i) % 2][:, tile(j)],
                                       m.ssb[a % 2][:, tile(4 * i + j)], m.ident)
                ins.then_inc(G["pt_done"], 1)

            turn(0)
            for i in range(len(chunks)):
                if i + 1 < len(chunks):
                    turn(i + 1)
                need(G["pt_ready"], n0 + i + 1)
                if i == 0:
                    need(G["qk_ready"], ropes_to(s - 1))
                    need(G["proj_read"], 12 * (q + 1))
                    need(G["y_done"], a)
                for j, (g, k) in enumerate(chunks[i]):
                    last = i == len(chunks) - 1 and j == len(chunks[i]) - 1
                    ins = pe.matmul(banks[2][:, 256:256 + HD], m.pt[:, tile(4 * i + j)],
                                    m.v[q % 2][:, k, g, HD * hh:HD * hh + HD],
                                    start=(i == 0 and j == 0), stop=last)
            ins.then_inc(G["pv_done"], 1)
        if u and u[0] == "ret":
            _, hp, k, _ = u
            r = RET_UNITS.index(u)
            need(G["sd_ready"], 4 * (r + 1))
            need(G["rn_ready"], r)
            need(G["proj_read"], 48 + 8 * (hp + 1))
            for t in range(T):
                for kt in range(T):
                    ins = pe.matmul(banks[7][:, tile(t)], m.sd[:, kt, tile(t)],
                                    m.rv[hp % 2][:, kt, tile(k)], start=(kt == 0), stop=(kt == T - 1))
            ins.then_inc(G["ro_done"], 1)


def act_mixer(nc, act, A, m, G, banks):
    need = Need(act)
    step = Tick(act, G["act_step"])
    for s in range(NSTEP):
        if s < NPROJ:
            kind, a, b, t = STEPS[s]
            bank = banks[s % 2]
            need(G["proj_done"], s + 1)
            if kind in ("A", "R1"):
                need(G["rope_read"], ropes_to(s))
            if kind == "A":
                need(G["pv_done"], 8 * (a - 1))
                act.activation(m.v[a % 2][:, t, b, :], bank[:, 2 * HP2:3 * HP2], ACT.Copy)\
                   .then_inc(G["proj_read"], 1)
            if kind == "R1":
                need(G["ro_done"], 2 * (a - 1))
                act.activation(m.rv[a % 2][:, t, tile(0)], bank[:, 2 * P:3 * P], ACT.Copy)\
                   .then_inc(G["proj_read"], 1)
            if kind == "R2":
                need(G["ry_ready"], 2 * (a - 1))
                act.activation(m.rv[a % 2][:, t, tile(1)], bank[:, 0:P], ACT.Copy)
                act.activation(m.rg[a % 2][:, t, :], bank[:, P:3 * P], ACT.Silu)\
                   .then_inc(G["proj_read"], 1)
            if kind == "G":
                j = 2 * a + b
                need(G["smalls_in"], 32)
                act.activation(m.gates[:, j, :], bank[:, :], ACT.Sigmoid, bias=m.gate_b[:, j:j + 1])\
                   .then_inc(G["proj_read"], 1)
        if s - 1 in ROPES:
            n = ROPES.index(s - 1)
            kind, a, b, t = STEPS[s - 1]
            need(G["t_done"], n + 1)
            src = banks[2][:, 0:2 * P].rearrange("p (i c) -> p i c", i=2)
            if kind == "A":
                need(G["s_done"], 8 * (a - 1))
                dst = m.qk[a % 2][:, b, :, tile(t)]
            else:
                need(G["rs_done"], 8 * (a - 1))
                dst = m.rqk[a % 2][:, :, tile(t)]
            act.activation(dst, src, ACT.Copy).then_inc(G["qk_ready"], 1)
        u = UNITS.get(s - 1)
        if u and u[0] == "att":
            a = att_index(u)
            n0 = chunks_before(a)
            need(G["pv_done"], a)
            for i, ch in enumerate(att_chunks(u[3])):
                need(G["pt_done"], n0 + i + 1)
                act.activation(m.pt[:, 4 * i * P:(4 * i + len(ch)) * P],
                               banks[6 + (n0 + i) % 2][:, 0:P * len(ch)], ACT.Copy)\
                   .then_inc(G["pt_ready"], 1)
        u = UNITS.get(s)
        if u and u[0] == "att":
            a = att_index(u)
            n = P * len(att_blocks(u[3]))
            need(G["negm_ready"], a + 1)
            act.activation(m.ssb[a % 2][:, 0:n], m.ssb[a % 2][:, 0:n], ACT.Exp, scale=HD ** -0.5,
                           bias=m.negm[a % 2], accum_out=m.den[a % 2]).then_inc(G["exp_done"], 1)
        u = UNITS.get(s + 1)
        if u and u[0] == "ret":
            r = RET_UNITS.index(u)
            need(G["lg_ready"], 1)
            need(G["dt_ready"], r)
            for i in range(2):
                act.activation(m.e12[:, i, :], m.tabs[:, i, :], ACT.Exp, scale=m.lg[:, i, r:r + 1])\
                   .then_inc(G["e_ready"], 1)


def dve_mixer(nc, dve, m, G, banks):
    need = Need(dve)
    step = Tick(dve, G["dve_step"])
    dve.wait_ge(G["tables_in"], 16 * 4)
    x = m.decay.rearrange("p a b -> p (a b)")
    neg, z, r, r2, s, lo = (m.ls[:, i, :] for i in range(6))
    step.wait(step(dve.tensor_scalar(neg, x, -1.0, None, ALU.mult)))
    dve.tensor_tensor(neg, neg, x, ALU.min).then_inc(G["lg_half"], 1)
    step(dve.tensor_scalar(lo, x, 0.0, None, ALU.min))
    dve.wait_ge(G["lg_half"], 2)
    step.wait(step(dve.tensor_scalar(r2, z, 2.0, None, ALU.add)))
    step.wait(step(dve.reciprocal(r2, r2)))
    step.wait(step(dve.tensor_tensor(r, z, r2, ALU.mult)))
    step.wait(step(dve.tensor_tensor(r2, r, r, ALU.mult)))
    step.wait(step(dve.tensor_scalar(s, r2, 1.0 / 19, 1.0 / 17, ALU.mult, ALU.add)))
    for k in (15, 13, 11, 9, 7, 5, 3, 1):
        step.wait(step(dve.tensor_tensor(s, s, r2, ALU.mult)))
        step.wait(step(dve.tensor_scalar(s, s, 1.0 / k, None, ALU.add)))
    step.wait(step(dve.tensor_tensor(s, s, r, ALU.mult)))
    dve.scalar_tensor_tensor(m.lg.rearrange("p a b -> p (a b)"), s, -2.0, lo, ALU.mult, ALU.add)\
       .then_inc(G["lg_ready"], 1)

    for sn in range(NSTEP):
        if sn < NPROJ and sn in ROPES:
            n = ROPES.index(sn)
            t = STEPS[sn][3]
            x = banks[sn % 2][:, 0:2 * HP2].rearrange("p (h two d) -> p h two d", h=4, two=2)
            need(G["proj_done"], sn + 1)
            need(G["rot_ready"], n - 1)
            cos = m.cos[:, t, :].unsqueeze(1).unsqueeze(1).broadcast_to([P, 4, 2, HD // 2])
            sin = m.sin[:, t, :].unsqueeze(1).broadcast_to([P, 4, HD // 2])
            nsin = m.nsin[:, t, :].unsqueeze(1).broadcast_to([P, 4, HD // 2])
            dve.tensor_tensor(m.ra[n % 2], x, cos, ALU.mult)
            dve.tensor_tensor(m.rb[n % 2][:, :, 0, :], x[:, :, 1, :], nsin, ALU.mult)
            dve.tensor_tensor(m.rb[n % 2][:, :, 1, :], x[:, :, 0, :], sin, ALU.mult)\
               .then_inc(G["rope_read"], 1)
        u = UNITS.get(sn)
        if u and u[0] == "att":
            a, t = att_index(u), u[3]
            need(G["s_done"], a + 1)
            need(G["mask_in"], 16)
            need(G["pt_done"], chunks_before(max(a - 1, 0)))
            at = 0
            for g in range(AG):
                ks = att_keys(g, t)
                n = P * len(ks)
                c0 = WOFF + (ks[0] - t) * P
                k = step(dve.tensor_tensor_reduce(
                    out=m.ssb[a % 2][:, at:at + n], in0=banks[3 + g][:, 0:n],
                    in1=m.masks[:, g, c0:c0 + n], scale=1.0, scalar=-3.0e38, op0=ALU.add,
                    op1=ALU.max, accum_out=m.mx[a % 2][:, g:g + 1])) if g < 2 else \
                    dve.tensor_tensor_reduce(
                    out=m.ssb[a % 2][:, at:at + n], in0=banks[3 + g][:, 0:n],
                    in1=m.masks[:, g, c0:c0 + n], scale=1.0, scalar=-3.0e38, op0=ALU.add,
                    op1=ALU.max, accum_out=m.mx[a % 2][:, g:g + 1]).then_inc(G["s_masked"], 1)
                at += n
            step.wait(step.n)
            dve.wait_ge(G["s_masked"], a + 1)
            step.wait(step(dve.tensor_reduce(m.mx[a % 2][:, 3:4], m.mx[a % 2][:, 0:3], AX.X, ALU.max)))
            need(G["exp_done"], a - 1)
            dve.tensor_scalar(m.negm[a % 2], m.mx[a % 2][:, 3:4], -HD ** -0.5, None, ALU.mult)\
               .then_inc(G["negm_ready"], 1)
        if u and u[0] == "ret":
            r = RET_UNITS.index(u)
            need(G["dt_ready"], r + 1)
            need(G["ro_done"], r)
            need(G["pt_done"], chunks_before(len(ATT_UNITS)))
            for kt in range(T):
                need(G["rs_done"], 4 * r + kt + 1)
                c0 = WOFF - kt * P
                dve.scalar_tensor_tensor(m.sd[:, kt, :], banks[3 + kt][:, :], RK ** -0.5,
                                         m.dt[r % 2][:, c0:c0 + S], ALU.mult, ALU.mult)\
                   .then_inc(G["sd_ready"], 1)
        u = UNITS.get(sn - 1)
        if u and u[0] == "att":
            a, (_, q, hh, t) = att_index(u), u
            need(G["exp_done"], a + 1)
            k = step(dve.reciprocal(m.rden[a % 2], m.den[a % 2]))
            need(G["pv_done"], a + 1)
            step.wait(k)
            c0 = (2 * q + hh) * HD
            dve.tensor_scalar(m.y_att[:, t, c0:c0 + HD], banks[2][:, 256:256 + HD],
                              m.rden[a % 2], None, ALU.mult).then_inc(G["y_done"], 1)
        if u and u[0] == "ret":
            r = RET_UNITS.index(u)
            need(G["ro_done"], r + 1)
            for t in range(T):
                k = step(dve.bn_stats(m.bst[:, t, :], banks[7][:, tile(t)]))
            step.wait(k)
            need(G["rn_ready"], r)
            need(G["rstd_ready"], r)
            for t in range(T):
                ins = dve.bn_aggr(m.bmv[:, t, :], m.bst[:, t, :])
                if t < T - 1:
                    step(ins)
            ins.then_inc(G["var_ready"], 1)
            step.wait(step.n)
            dve.wait_ge(G["var_ready"], r + 1)
            need(G["rstd_ready"], r + 1)
            need(G["ry_ready"], r)
            for t in range(T):
                ins = dve.tensor_scalar(m.rn[:, t, :], banks[7][:, tile(t)], m.bmv[:, t, 0:1],
                                        m.rstd[:, t:t + 1], ALU.subtract, ALU.mult)
                if t < T - 1:
                    step(ins)
            ins.then_inc(G["rn_ready"], 1)


def pool_mixer(nc, pool, A, m, G):
    need = Need(pool)
    step = Tick(pool, G["pool_step"])
    pool.memset(m.half, -0.5).then_inc(G["pool_step"], 1)
    step.n += 1
    for s in range(NSTEP):
        if s < NPROJ and s in ROPES:
            n = ROPES.index(s)
            need(G["rope_read"], n + 1)
            need(G["t_done"], n - 1)
            pool.tensor_tensor(m.rot[n % 2], m.ra[n % 2].rearrange("p a b c -> p (a b c)"),
                               m.rb[n % 2].rearrange("p a b c -> p (a b c)"), ALU.add)\
                .then_inc(G["rot_ready"], 1)
        u = UNITS.get(s + 1)
        if u and u[0] == "ret":
            r = RET_UNITS.index(u)
            need(G["e_ready"], 2 * (r + 1))
            need(G["sd_ready"], 4 * (r - 1))
            step.wait(step(pool.tensor_tensor(m.dt[r % 2], m.e12[:, 0, :], m.e12[:, 1, :], ALU.mult)))
            pool.tensor_tensor(m.dt[r % 2], m.dt[r % 2], m.tabs[:, 2, :], ALU.add)\
                .then_inc(G["dt_ready"], 1)
        u = UNITS.get(s - 1)
        if u and u[0] == "ret":
            r, (_, hp, k, _) = RET_UNITS.index(u), u
            need(G["var_ready"], r + 1)
            step.wait(step(pool.tensor_scalar(m.rstd, m.bmv[:, :, 1], EPS, None, ALU.add)))
            pool.tensor_tensor(m.rstd, m.rstd, m.half.broadcast_to([P, T]), ALU.pow)\
                .then_inc(G["rstd_ready"], 1)
            need(G["rn_ready"], r + 1)
            need(G["proj_read"], 48 + 8 * (hp + 1))
            need(G["smalls_in"], 32)
            step.wait(step(pool.tensor_tensor(m.rn2, m.rn, m.rg[hp % 2][:, :, tile(k)], ALU.mult)))
            w = m.gnw[:, tile(r)].unsqueeze(1).broadcast_to([P, T, RV])
            pool.tensor_tensor(m.y_ret[:, :, tile(r)], m.rn2, w, ALU.mult).then_inc(G["ry_ready"], 1)


def mixer_block(nc, m, G, banks, A):
    with nc.Block() as block:

        @block.sync
        def _(sp):
            consts = A["consts"]
            cols, _ = const_columns()

            def table(dst, name, sem):
                a, n = cols[name]
                sp.dma_start(dst, consts[:, a:a + n]).then_inc(G[sem], 16)

            for i, name in enumerate(("ret_decay_fwd", "ret_decay_bwd")):
                sp.dma_start(m.decay[:, i, :], A[name][0].partition_broadcast(P)).then_inc(G["tables_in"], 16)
            sp.dma_start(m.trig, consts[:, cols["cos"][0]:cols["cos"][0] + 3 * T * HD // 2])\
              .then_inc(G["tables_in"], 16)
            sp.dma_start(m.tabs.rearrange("p a b -> p (a b)"),
                         consts[:, cols["fwd"][0]:cols["fwd"][0] + 3 * WB]).then_inc(G["tables_in"], 16)
            sp_first(sp, A, m, G)
            sp.dma_start(m.masks.rearrange("p a b -> p (a b)"),
                         consts[:, cols["mask0"][0]:cols["mask0"][0] + 3 * WB]).then_inc(G["mask_in"], 16)
            sp.dma_start(m.gnw, A["ret_gn_w"][0].partition_broadcast(P)).then_inc(G["smalls_in"], 16)
            sp.dma_start(m.gate_b, A["b_branch_gate"][0].rearrange("(a p) -> p a", p=P),
                         allow_slow_non_contiguous=True).then_inc(G["smalls_in"], 16)
            sp_mixer(sp, A, m, G)

        @block.tensor
        def _(pe):
            pe_mixer(nc, pe, m, G, banks)

        @block.scalar
        def _(act):
            act.wait_ge(G["lg_half"], 1)
            act.activation(m.ls[:, 1, :], m.ls[:, 0, :], ACT.Exp).then_inc(G["lg_half"], 1)
            act_mixer(nc, act, A, m, G, banks)

        @block.vector
        def _(dve):
            dve_mixer(nc, dve, m, G, banks)

        @block.gpsimd
        def _(pool):
            pool.wait_ge(G["tables_in"], 64)
            pool_mixer(nc, pool, A, m, G)


NORM_SEMS = ["norm_w_in", "stat_ready", "norm_rstd", "scaled", "norm_out", "turned", "aT_ready", "norm_step", "norm_pool_step"]


def norm_views(m, at):
    sp = Space(m.arena, at)
    m.nw, m.nb = sp(D), sp(D)
    m.nj = sp(2, D)
    m.nss, m.nrs, m.nt = sp(T), sp(T), sp(T)
    m.nst, m.nmv = sp(T, 12), sp(T, 2)
    m.nhalf = sp(1)
    m.ns = sp(T, D)
    m.after_norm = sp.at


def norm_block(nc, m, G, banks, v, kind, dst, w, b=None, eps=EPS, nln=0):
    n_in = G["norm_w_at"]
    ndma = 1 + (b is not None)
    G["norm_w_at"] = n_in + 16 * ndma

    with nc.Block() as block:

        @block.sync
        def _(sp):
            sp.dma_start(m.nw, w.partition_broadcast(P)).then_inc(G["norm_w_in"], 16)
            if b is not None:
                sp.dma_start(m.nb, b.partition_broadcast(P)).then_inc(G["norm_w_in"], 16)

        @block.scalar
        def _(act):
            for t in range(T):
                if kind == "rms":
                    if t >= 2:
                        act.wait_ge(G["stat_ready"], T * v + t - 1)
                    act.activation(m.nj[:, t % 2, :], m.h[:, t, :], ACT.Square,
                                   accum_out=m.nss[:, t:t + 1]).then_inc(G["stat_ready"], 1)
            for i in range(2 * T):
                act.wait_ge(G["turned"], 2 * T * v + i + 1)
                act.activation(m.aT[:, 4 * (i % 2):4 * (i % 2) + 4, tile(i // 2)],
                               banks[i % 4][:, :].rearrange("p (a c) -> p a c", a=4), ACT.Copy)\
                   .then_inc(G["aT_ready"], 1)

        @block.gpsimd
        def _(pool):
            pool.memset(m.nhalf, -0.5).then_inc(G["norm_pool_step"], 1)
            n = G["pool_at"] + 1
            pool.wait_ge(G["norm_pool_step"], n)
            for t in range(T):
                pool.wait_ge(G["stat_ready"], T * v + t + 1)
                if kind == "rms":
                    ins = pool.tensor_scalar(m.nt[:, t:t + 1], m.nss[:, t:t + 1], 1.0 / D, eps, ALU.mult, ALU.add)
                else:
                    ins = pool.tensor_scalar(m.nt[:, t:t + 1], m.nmv[:, t, 1:2], eps, None, ALU.add)
                ins.then_inc(G["norm_pool_step"], 1)
                n += 1
                pool.wait_ge(G["norm_pool_step"], n)
                pool.tensor_tensor(m.nrs[:, t:t + 1], m.nt[:, t:t + 1], m.nhalf, ALU.pow)\
                    .then_inc(G["norm_rstd"], 1)
            if kind == "ln":
                for t in range(T):
                    pool.wait_ge(G["scaled"], T * nln + t + 1)
                    pool.wait_ge(G["norm_w_in"], n_in + 16 * ndma)
                    pool.tensor_tensor(dst[:, t, :], m.ns[:, t, :], m.nb, ALU.add)\
                        .then_inc(G["norm_out"], 1)
            G["pool_at"] = n

        @block.vector
        def _(dve):
            n = G["dve_at"]
            if kind == "ln":
                for t in range(T):
                    for i in range(2):
                        dve.bn_stats(m.nst[:, t, 6 * i:6 * i + 6], m.h[:, t, 512 * i:512 * i + 512])\
                           .then_inc(G["norm_step"], 1)
                    n += 2
                for t in range(T):
                    dve.wait_ge(G["norm_step"], n - 2 * (T - 1 - t))
                    dve.bn_aggr(m.nmv[:, t, :], m.nst[:, t, :]).then_inc(G["stat_ready"], 1)
            dve.wait_ge(G["norm_w_in"], n_in + 16 * ndma)
            for t in range(T):
                dve.wait_ge(G["norm_rstd"], T * v + t + 1)
                if kind == "rms":
                    dve.scalar_tensor_tensor(dst[:, t, :], m.h[:, t, :], m.nrs[:, t:t + 1], m.nw,
                                             ALU.mult, ALU.mult).then_inc(G["norm_out"], 1)
                else:
                    dve.tensor_scalar(m.nj[:, t % 2, :], m.h[:, t, :], m.nmv[:, t, 0:1],
                                      m.nrs[:, t:t + 1], ALU.subtract, ALU.mult)\
                       .then_inc(G["norm_step"], 1)
                    n += 1
                    dve.wait_ge(G["norm_step"], n)
                    dve.tensor_tensor(m.ns[:, t, :], m.nj[:, t % 2, :], m.nw, ALU.mult)\
                       .then_inc(G["scaled"], 1)
            G["dve_at"] = n

        @block.tensor
        def _(pe):
            for i in range(2 * T):
                t = i // 2
                pe.wait_ge(G["norm_out"], T * v + t + 1)
                if i >= 4:
                    pe.wait_ge(G["aT_ready"], 2 * T * v + i - 3)
                for j in range(4):
                    ins = pe.transpose(banks[i % 4][:, tile(j)], dst[:, t, tile(4 * (i % 2) + j)],
                                       m.ident)
                ins.then_inc(G["turned"], 1)


MERGE_SEMS = ["y_turned", "yT_ready", "branch_done", "gated", "mT_ready", "mix_done", "mix_added",
              "x_again"] + [f"merge_in{i}" for i in range(NSLOT)]


def merge_memory(m):
    at = m.rqk_at
    m.yT = Space(m.arena, at)(12, S)
    m.g1 = [Space(m.arena, m.dt_at + 2 * S * i)(2, S) for i in range(2)]
    m.mring = [Space(m.arena, m.ring_at + KT * CW * i)(12, 256) for i in range(NSLOT)]
    m.mT = m.aT


def merge_block(nc, m, G, banks, A):
    merge_memory(m)
    with nc.Block() as block:

        @block.sync
        def _(sp):
            wa = A["w_attn_branch"][0].rearrange("(k p) n -> p k n", p=P)
            wr = A["w_ret_branch"][0].rearrange("(k p) n -> p k n", p=P)
            wo = A["w_out"][0].rearrange("(k p) n -> p k n", p=P)
            for c in range(8):
                if 3 <= c < 7:
                    sp.wait_ge(G["branch_done"], 4 * (c - 3 + 1))
                if c == 7:
                    sp.wait_ge(G["mix_done"], T)
                cs = slice(256 * (c % 4), 256 * (c % 4) + 256)
                if c < 4:
                    sp.dma_start(m.mring[c % 3][:, 0:4, :], wa[:, :, cs]).then_inc(G[f"merge_in{c % 3}"], 16)
                    sp.dma_start(m.mring[c % 3][:, 4:12, :], wr[:, :, cs]).then_inc(G[f"merge_in{c % 3}"], 16)
                else:
                    sp.dma_start(m.mring[c % 3][:, 0:8, :], wo[:, :, cs]).then_inc(G[f"merge_in{c % 3}"], 16)
            sp.dma_start(m.h, A["x"][0].rearrange("(t p) n -> p t n", p=P)).then_inc(G["x_again"], 16)

        def slot_in(c):
            return 16 * sum(2 if i < 4 else 1 for i in range(c % 3, c + 1, 3))

        @block.tensor
        def _(pe):
            for i in range(3 * T):
                t, k = i // 3, i % 3
                if i >= 4:
                    pe.wait_ge(G["yT_ready"], i - 3)
                src = m.y_att[:, t, :] if k == 0 else m.y_ret[:, t, 512 * (k - 1):512 * k]
                for j in range(4):
                    ins = pe.transpose(banks[i % 4][:, tile(j)], src[:, tile(j)], m.ident)
                ins.then_inc(G["y_turned"], 1)
            for j in range(KT):
                c = j // 2
                pe.wait_ge(G[f"merge_in{c % 3}"], slot_in(c))
                pe.wait_ge(G["yT_ready"], 3 * T)
                for i, (k0, k1) in enumerate(((0, 4), (4, 12))):
                    if j >= 2:
                        pe.wait_ge(G["gated"], 2 * (j - 2) + i + 1)
                    for k in range(k0, k1):
                        ins = pe.matmul(banks[2 * (j % 2) + i][:, :], m.mring[c % 3][:, k, tile(j % 2)],
                                        m.yT[:, k, :], start=(k == k0), stop=(k == k1 - 1))
                    ins.then_inc(G["branch_done"], 1)
            for n in range(4 * T):
                c, t = n // T, n % T
                pe.wait_ge(G[f"merge_in{(4 + c) % 3}"], slot_in(4 + c))
                pe.wait_ge(G["mT_ready"], KT)
                if n >= 4:
                    pe.wait_ge(G["mix_added"], n - 3)
                for k in range(KT):
                    ins = pe.matmul(banks[4 + n % 4][:, 0:256], m.mT[:, k, tile(t)],
                                    m.mring[(4 + c) % 3][:, k, :], start=(k == 0), stop=(k == KT - 1))
                ins.then_inc(G["mix_done"], 1)

        @block.scalar
        def _(act):
            for i in range(3 * T):
                t, k = i // 3, i % 3
                act.wait_ge(G["y_turned"], i + 1)
                act.activation(m.yT[:, 4 * k:4 * k + 4, tile(t)],
                               banks[i % 4][:, :].rearrange("p (a c) -> p a c", a=4), ACT.Copy)\
                   .then_inc(G["yT_ready"], 1)

        @block.vector
        def _(dve):
            for j in range(KT):
                for i in range(2):
                    dve.wait_ge(G["branch_done"], 2 * j + i + 1)
                    if j >= 2:
                        dve.wait_ge(G["mT_ready"], j - 1)
                    dve.tensor_tensor(m.g1[j % 2][:, i, :], banks[2 * (j % 2) + i][:, :],
                                      m.gates[:, KT * i + j, :], ALU.mult).then_inc(G["gated"], 1)
            dve.wait_ge(G["x_again"], 16)
            for n in range(4 * T):
                c, t = n // T, n % T
                dve.wait_ge(G["mix_done"], n + 1)
                hs = m.h[:, t, 256 * c:256 * c + 256]
                dve.tensor_tensor(hs, hs, banks[4 + n % 4][:, 0:256], ALU.add).then_inc(G["mix_added"], 1)

        @block.gpsimd
        def _(pool):
            for j in range(KT):
                pool.wait_ge(G["gated"], 2 * j + 2)
                pool.tensor_tensor(m.mT[:, j, :], m.g1[j % 2][:, 0, :], m.g1[j % 2][:, 1, :], ALU.add)\
                    .then_inc(G["mT_ready"], 1)


NE, NG, GE = 64, 8, 8
CAP = 32
MAIN = NE
MORE = 2 * S // CAP
FF = 512
ROUTER_SEMS = ["rw_in", "logits_done", "logits_ready", "r_exp_in", "r_exp", "assigned", "counted",
               "routed", "zeroed", "more_zeroed", "eb_sent", "eb_in", "r_step"]
MOE_SEMS = ["up_done", "hs_ready", "hid_ready", "ht_turned", "ht_ready", "down_done", "yo_ready",
            "y_sent0", "y_sent1", "g_ready", "gather_done", "xt_ready", "g_step",
            "ov_in", "ov_g", "ov_gathered", "ov_xt", "ov_up", "ov_hs", "ov_hid", "ov_turned",
            "ov_ht", "ov_down", "ov_y", "ov_sent", "ov_step"] + [f"e_in{i}" for i in range(6)]
COMB_SEMS = [f"y_in{i}" for i in range(16)] + ["combined"]


def moe_memory(arena):
    m = persistent(arena)
    sp = Space(arena, m.free)
    m.hn = sp(T, D)
    m.rw = sp(KT, NG + NE)
    m.rb = sp(NG + NE)
    m.iota = sp(P)
    m.piota = sp(1)
    m.before, m.ones = sp(P), sp(P)
    m.lg = sp(T, NG + NE)
    m.r8 = [sp(T, 8) for _ in range(8)]
    m.r1 = [sp(T) for _ in range(12)]
    m.prod = sp(T, NG * GE)
    m.pick = [sp(T, NE) for _ in range(2)]
    m.both = sp(T, NE)
    m.pos = sp(T, NE)
    m.e64 = [sp(NE) for _ in range(5)]
    m.k8 = [sp(2, T) for _ in range(6)]
    m.yrel = sp(2, T)
    m.gate = sp(2, T)
    m.yidx = sp(4, T)
    m.yidx_i = sp(4, T).bitcast(i32)
    m.misc = sp(4)
    m.misc_i = sp(4).bitcast(i32)
    m.eb_i = sp(MORE).bitcast(i32)
    m.G = sp(T, P)
    m.G1 = sp(T, P)
    m.xt = sp(KT, P)
    m.hs, m.hid = sp(FF), sp(FF)
    m.ht = sp(FF // P, 2 * CAP)
    m.yo = [sp(512) for _ in range(2)]
    m.zero = sp(512)
    m.norm_at = sp.at
    m.w = [sp(KT * FF) for _ in range(6)]
    m.yg = [Space(arena, m.norm_at + 512 * i)(512) for i in range(16)]
    return m


def router_block(nc, m, G, banks, A, eb_dram, y_slots):
    cols, _ = const_columns()
    consts = A["consts"]
    with nc.Block() as block:

        @block.sync
        def _(sp):
            def load(dst, src, slow=False):
                sp.dma_start(dst, src, allow_slow_non_contiguous=True).then_inc(G["rw_in"], 16)

            load(m.rw[:, :, 0:NG], A["moe_w_group"][0].rearrange("(k p) n -> p k n", p=P), True)
            load(m.rw[:, :, NG:], A["moe_w_expert"][0].rearrange("(k p) n -> p k n", p=P))
            load(m.rb[:, 0:NG], A["moe_b_group"][0].partition_broadcast(P))
            load(m.rb[:, NG:], A["moe_b_expert"][0].partition_broadcast(P))
            for dst, name in ((m.iota, "iota"), (m.before, "before"), (m.ones, "ones"), (m.piota, "piota")):
                load(dst, consts[:, cols[name][0]:cols[name][0] + cols[name][1]])
            sp.wait_ge(G["routed"], 1)
            sp.dma_start(eb_dram.rearrange("a b -> b a"), m.misc_i[0:MORE, 0:1]).then_inc(G["eb_sent"], 16)
            sp.wait_ge(G["eb_sent"], 16)
            sp.dma_start(m.eb_i[0:1, :], eb_dram).then_inc(G["eb_in"], 16)
            sp.wait_ge(G["eb_in"], 16)

        @block.tensor
        def _(pe):
            pe.wait_ge(G["rw_in"], 128)
            for t in range(T):
                for k in range(KT):
                    ins = pe.matmul(banks[t][:, 0:NG + NE], m.aT[:, k, tile(t)], m.rw[:, k, :],
                                    start=(k == 0), stop=(k == KT - 1))
                ins.then_inc(G["logits_done"], 1)
            pe.wait_ge(G["assigned"], 1)
            for t in range(T):
                for u in range(t + 1):
                    pe.matmul(banks[4][:, t * NE:(t + 1) * NE], m.ones if u < t else m.before,
                              m.both[:, u, :], start=(u == 0), stop=(u == t))
            for u in range(T):
                ins = pe.matmul(banks[5][:, 0:NE], m.ones, m.both[:, u, :], start=(u == 0), stop=(u == T - 1))
            ins.then_inc(G["counted"], 1)

        @block.gpsimd
        def _(pool):
            pool.memset(m.hid, 0.0).then_inc(G["zeroed"], 1)
            pool.memset(m.zero, 0.0).then_inc(G["zeroed"], 1)
            pool.wait_ge(G["zeroed"], 2)
            pool.dma_start(y_slots[MAIN * 2 * CAP:, :].rearrange("(a p) n -> p a n", p=P),
                           m.zero.unsqueeze(1).broadcast_to([P, MORE * 2 * CAP // P, 512]))\
                .then_inc(G["more_zeroed"], 16)
            pool.wait_ge(G["more_zeroed"], 16)

        @block.scalar
        def _(act):
            act.wait_ge(G["r_exp_in"], 1)
            act.activation(m.r8[1], m.r8[0], ACT.Exp).then_inc(G["r_exp"], 1)
            act.wait_ge(G["r_exp_in"], 2)
            act.activation(m.r1[3], m.r1[2], ACT.Exp).then_inc(G["r_exp"], 1)

        @block.vector
        def _(dve):
            step = Tick(dve, G["r_step"])

            def do(ins):
                step.wait(step(ins))

            def over(x, n):
                return x.unsqueeze(2).broadcast_to([P, T, n])

            def first(x, top, oh, idx, tmp):
                do(dve.tensor_reduce(top, x, AX.X, ALU.max))
                do(dve.tensor_tensor(tmp, x, over(top, 8), ALU.is_equal))
                i8 = m.iota[:, 0:8].unsqueeze(1).broadcast_to([P, T, 8])
                do(dve.scalar_tensor_tensor(tmp, tmp, -8.0, i8, ALU.mult, ALU.add))
                do(dve.tensor_reduce(idx, tmp, AX.X, ALU.min))
                do(dve.tensor_scalar(idx, idx, 8.0, None, ALU.add))
                do(dve.tensor_tensor(oh, i8, over(idx, 8), ALU.is_equal))

            dve.wait_ge(G["rw_in"], 128)
            for t in range(T):
                dve.wait_ge(G["logits_done"], t + 1)
                ins = dve.tensor_tensor(m.lg[:, t, :], banks[t][:, 0:NG + NE], m.rb, ALU.add)
                step(ins)
            step.wait(T)
            gl = m.lg[:, :, 0:NG]
            gmax, gidx, gw = m.r1[0], m.r1[1], m.r1[4]
            first(gl, gmax, m.r8[2], gidx, m.r8[3])
            step(dve.tensor_tensor(m.r8[0], gl, over(gmax, 8), ALU.subtract))
            step.wait(step.n)
            dve.sem_inc(G["r_exp_in"], 1)
            el = m.lg[:, :, NG:].rearrange("p t (g j) -> p t g j", g=NG)
            pr = m.prod.rearrange("p t (g j) -> p t g j", g=NG)
            do(dve.tensor_tensor(pr, el, m.r8[2].unsqueeze(3).broadcast_to([P, T, NG, GE]), ALU.mult))
            sel, oh1, oh2, tmp = m.r8[4], m.r8[5], m.r8[6], m.r8[7]
            do(dve.tensor_reduce(sel, pr.rearrange("p t g j -> p t j g"), AX.X, ALU.add))
            m1, i1, m2, i2 = m.r1[5], m.r1[6], m.r1[7], m.r1[8]
            first(sel, m1, oh1, i1, tmp)
            do(dve.scalar_tensor_tensor(sel, oh1, NEG, sel, ALU.mult, ALU.add))
            first(sel, m2, oh2, i2, tmp)
            do(dve.tensor_tensor(m.r1[2], m2, m1, ALU.subtract))
            dve.sem_inc(G["r_exp_in"], 1)
            dve.wait_ge(G["r_exp"], 2)
            do(dve.tensor_reduce(gw, m.r8[1], AX.X, ALU.add))
            do(dve.tensor_scalar(m.r1[9], m.r1[3], 1.0, None, ALU.add))
            do(dve.tensor_tensor(gw, gw, m.r1[9], ALU.mult))
            do(dve.reciprocal(m.gate[:, 0, :], gw))
            do(dve.tensor_tensor(m.gate[:, 1, :], m.gate[:, 0, :], m.r1[3], ALU.mult))
            eid = m.k8[0]
            for k, i in enumerate((i1, i2)):
                do(dve.scalar_tensor_tensor(eid[:, k, :], gidx, float(GE), i, ALU.mult, ALU.add))
                i64 = m.iota[:, 0:NE].unsqueeze(1).broadcast_to([P, T, NE])
                do(dve.tensor_tensor(m.pick[k], i64, over(eid[:, k, :], NE), ALU.is_equal))
            step(dve.tensor_tensor(m.both, m.pick[0], m.pick[1], ALU.add))
            step.wait(step.n)
            dve.sem_inc(G["assigned"], 1)
            dve.wait_ge(G["counted"], 1)
            pos = banks[4][:, 0:T * NE].rearrange("p (t e) -> p t e", t=T)
            rank, ost, q, row, blk = (m.k8[i] for i in range(1, 6))
            do(dve.tensor_copy(m.pos, pos))
            do(dve.tensor_copy(m.e64[0], banks[5][:, 0:NE]))
            do(dve.memset(m.e64[1], 0.0))
            do(dve.memset(m.e64[4], 0.0))
            for j in range(1, S // CAP):
                do(dve.scalar_tensor_tensor(m.e64[1], m.e64[0], float(CAP * j), m.e64[1], ALU.is_gt, ALU.add))
            do(dve.tensor_tensor_scan(m.e64[2], m.e64[1], m.e64[4], 0.0, ALU.add, ALU.add))
            do(dve.tensor_tensor(m.e64[3], m.e64[2], m.e64[1], ALU.subtract))
            prod = m.prod
            for k in range(2):
                do(dve.tensor_tensor(prod, m.pick[k], m.pos, ALU.mult))
                do(dve.tensor_reduce(rank[:, k, :], prod, AX.X, ALU.add))
                do(dve.tensor_tensor(prod, m.pick[k], m.e64[3].unsqueeze(1).broadcast_to([P, T, NE]), ALU.mult))
                do(dve.tensor_reduce(ost[:, k, :], prod, AX.X, ALU.add))
            do(dve.memset(q, 0.0))
            for j in range(1, S // CAP):
                do(dve.scalar_tensor_tensor(q, rank, float(CAP * j), q, ALU.is_ge, ALU.add))
            do(dve.scalar_tensor_tensor(row, q, -float(CAP), rank, ALU.mult, ALU.add))
            do(dve.tensor_tensor(ost, ost, q, ALU.add))
            do(dve.scalar_tensor_tensor(ost, ost, float(MAIN - 1), eid, ALU.add, ALU.subtract))
            do(dve.tensor_scalar(blk, q, 1.0, None, ALU.min))
            do(dve.tensor_tensor(blk, blk, ost, ALU.mult))
            do(dve.tensor_tensor(blk, blk, eid, ALU.add))
            do(dve.scalar_tensor_tensor(m.yrel, blk, float(CAP), row, ALU.mult, ALU.add))
            for half in range(2):
                y = m.yidx[:, 2 * half:2 * half + 2, :]
                do(dve.scalar_tensor_tensor(y, blk, 2.0 * CAP, row, ALU.mult, ALU.add))
                do(dve.tensor_scalar(y, y, float(CAP * half), None, ALU.add))
            do(dve.tensor_copy(m.yidx_i, m.yidx))
            do(dve.tensor_scalar(m.e64[4], m.e64[2], m.piota, None, ALU.is_le))
            do(dve.tensor_reduce(m.misc[:, 0:1], m.e64[4], AX.X, ALU.add))
            do(dve.tensor_scalar(m.misc[:, 0:1], m.misc[:, 0:1], float(NE - 1), None, ALU.min))
            do(dve.tensor_copy(m.misc[:, 1:2], m.e64[2][:, NE - 1:NE]))
            dve.tensor_copy(m.misc_i[:, 0:2], m.misc[:, 0:2]).then_inc(G["routed"], 1)


def moe_block(nc, m, G, banks, A, y_slots):
    w1, w3, w2 = A["moe_w1"][0], A["moe_w3"][0], A["moe_w2"][0]
    NIT = NE // 4
    turned = banks[2][:, :].rearrange("p (f c) -> p f c", f=FF // P)
    y_rows = y_slots

    def up_dst(slot):
        return m.w[slot].rearrange("p (k n) -> p k n", k=KT)

    def down_dst(slot):
        return m.w[slot].rearrange("p (k n) -> p k n", k=FF // P)

    def up_src(w, e):
        return w[bass.ds(e, 1), :, :].rearrange("a (k p) n -> p (a k) n", p=P)

    def down_src(e):
        return w2[bass.ds(e, 1), :, :].rearrange("a (k p) n -> p (a k) n", p=P)

    with nc.Block() as block:

        @block.sync
        def _(sp):
            with sp.Fori(0, NIT) as i:
                for pr in range(2):
                    sp.wait_ge(G["up_done"], 2 * i + pr + 1)
                    for e2 in range(2):
                        e = 4 * i + 2 * pr + e2
                        sp.dma_start(up_dst(2 * e2), up_src(w1, e)).then_inc(G[f"e_in{2 * e2}"], 16)
                        sp.dma_start(up_dst(2 * e2 + 1), up_src(w3, e)).then_inc(G[f"e_in{2 * e2 + 1}"], 16)
                    sp.wait_ge(G["down_done"], 2 * i + pr + 1)
                    for e2 in range(2):
                        e = 4 * i + 2 * pr + e2
                        sp.dma_start(down_dst(4 + e2), down_src(e)).then_inc(G[f"e_in{4 + e2}"], 16)
            n = sp.value_load(m.misc_i[0:1, 1:2], min_val=0, max_val=MORE - 1)
            with sp.If(n > 0):
                sp.wait_ge(G["up_done"], 2 * NIT + 1)
                sp.wait_ge(G["down_done"], 2 * NIT + 1)
                with sp.Fori(0, n) as j:
                    e = sp.value_load(m.eb_i[0:1, bass.ds(j, 1)], min_val=0, max_val=NE - 1)
                    sp.wait_ge(G["ov_down"], j + 1)
                    sp.dma_start(up_dst(0), up_src(w1, e)).then_inc(G["ov_in"], 16)
                    sp.dma_start(up_dst(1), up_src(w3, e)).then_inc(G["ov_in"], 16)
                    sp.dma_start(down_dst(4), down_src(e)).then_inc(G["ov_in"], 16)

        @block.tensor
        def _(pe):
            pe.sem_inc(G["up_done"], 1)
            pe.sem_inc(G["down_done"], 1)
            pe.sem_inc(G["ov_down"], 1)

            def gather():
                for d in range(KT):
                    for t in range(T):
                        ins = pe.matmul(banks[5 + d // 4][:, tile(d % 4)], m.hn[:, t, tile(d)],
                                        m.G[:, t, :], start=(t == 0), stop=(t == T - 1))
                    if d % 4 == 3:
                        ins.then_inc(G["gather_done"], 1)

            pe.wait_ge(G["g_ready"], 1)
            gather()
            with pe.Fori(0, NIT) as i:
                pe.wait_ge(G["xt_ready"], 2 * i + 2)
                for pr in range(2):
                    for s in range(4):
                        pe.wait_ge(G[f"e_in{s}"], 32 * i + 16 * pr + 16)
                    for k in range(KT):
                        for e2 in range(2):
                            for up in range(2):
                                q = 64 * up + 32 * e2
                                c = CAP * (2 * pr + e2)
                                ins = pe.matmul(banks[pr][q:q + CAP, :], m.xt[:, k, c:c + CAP],
                                                up_dst(2 * e2 + up)[:, k, :],
                                                start=(k == 0), stop=(k == KT - 1))
                    ins.then_inc(G["up_done"], 1)
                    pe.wait_ge(G["hid_ready"], 2 * i + pr + 1)
                    for f in range(FF // P):
                        ins = pe.transpose(banks[2][:, tile(f)], m.hid[:, tile(f)], m.ident)
                    ins.then_inc(G["ht_turned"], 1)
                    pe.wait_ge(G["ht_ready"], 2 * i + pr + 1)
                    pe.wait_ge(G["e_in4"], 32 * i + 16 * pr + 16)
                    pe.wait_ge(G["e_in5"], 32 * i + 16 * pr + 16)
                    pe.wait_ge(G["yo_ready"], 2 * i + pr + 1)
                    for f in range(FF // P):
                        for e2 in range(2):
                            for half in range(2):
                                q = 64 * e2 + 32 * half
                                ins = pe.matmul(banks[3 + pr][q:q + CAP, :],
                                                m.ht[:, f, CAP * e2:CAP * e2 + CAP],
                                                down_dst(4 + e2)[:, f, 512 * half:512 * half + 512],
                                                start=(f == 0), stop=(f == FF // P - 1))
                    ins.then_inc(G["down_done"], 1)
                pe.wait_ge(G["g_ready"], i + 2)
                gather()
            n = pe.value_load(m.misc_i[0:1, 1:2], min_val=0, max_val=MORE - 1)
            with pe.If(n > 0):
                pe.wait_ge(G["xt_ready"], 2 * NIT + 2)
                with pe.Fori(0, n) as j:
                    pe.wait_ge(G["ov_g"], j + 1)
                    for d in range(KT):
                        for t in range(T):
                            ins = pe.matmul(banks[5][:, CAP * d:CAP * d + CAP], m.hn[:, t, tile(d)],
                                            m.G[:, t, 0:CAP], start=(t == 0), stop=(t == T - 1))
                    ins.then_inc(G["ov_gathered"], 1)
                    pe.wait_ge(G["ov_xt"], j + 1)
                    pe.wait_ge(G["ov_in"], 48 * j + 48)
                    for k in range(KT):
                        for up in range(2):
                            ins = pe.matmul(banks[0][64 * up:64 * up + CAP, :], m.xt[:, k, 0:CAP],
                                            up_dst(up)[:, k, :], start=(k == 0), stop=(k == KT - 1))
                    ins.then_inc(G["ov_up"], 1)
                    pe.wait_ge(G["ov_hid"], j + 1)
                    for f in range(FF // P):
                        ins = pe.transpose(banks[2][:, tile(f)], m.hid[:, tile(f)], m.ident)
                    ins.then_inc(G["ov_turned"], 1)
                    pe.wait_ge(G["ov_ht"], j + 1)
                    for f in range(FF // P):
                        for half in range(2):
                            ins = pe.matmul(banks[3][32 * half:32 * half + CAP, :], m.ht[:, f, 0:CAP],
                                            down_dst(4)[:, f, 512 * half:512 * half + 512],
                                            start=(f == 0), stop=(f == FF // P - 1))
                    ins.then_inc(G["ov_down"], 1)

        @block.scalar
        def _(act):
            act.sem_inc(G["y_sent0"], 16)
            act.sem_inc(G["y_sent1"], 16)
            act.sem_inc(G["ov_sent"], 16)

            def xt_copy(n):
                for d in range(2):
                    act.wait_ge(G["gather_done"], n + d + 1)
                    act.activation(m.xt[:, 4 * d:4 * d + 4, :],
                                   banks[5 + d][:, :].rearrange("p (a c) -> p a c", a=4), ACT.Copy)\
                       .then_inc(G["xt_ready"], 1)

            xt_copy(0)
            with act.Fori(0, NIT) as i:
                for pr in range(2):
                    act.wait_ge(G["up_done"], 2 * i + pr + 2)
                    act.activation(m.hs[64:128, :], banks[pr][0:64, :], ACT.Silu).then_inc(G["hs_ready"], 1)
                    act.wait_ge(G["ht_turned"], 2 * i + pr + 1)
                    act.activation(m.ht, turned[:, :, 0:2 * CAP], ACT.Copy)\
                       .then_inc(G["ht_ready"], 1)
                    act.wait_ge(G["yo_ready"], 2 * i + pr + 3)
                    act.dma_start(y_rows[bass.ds(256 * i + 128 * pr, 128), :], m.yo[pr])\
                       .then_inc(G[f"y_sent{pr}"], 16)
                xt_copy(2 * i + 2)
            act.wait_ge(G["y_sent0"], 16 * NIT + 16)
            act.wait_ge(G["y_sent1"], 16 * NIT + 16)
            n = act.value_load(m.misc_i[0:1, 1:2], min_val=0, max_val=MORE - 1)
            with act.If(n > 0):
                with act.Fori(0, n) as j:
                    act.wait_ge(G["ov_gathered"], j + 1)
                    act.activation(m.xt[:, :, 0:CAP],
                                   banks[5][:, 0:KT * CAP].rearrange("p (a c) -> p a c", a=KT), ACT.Copy)\
                       .then_inc(G["ov_xt"], 1)
                    act.wait_ge(G["ov_up"], j + 1)
                    act.activation(m.hs[64:64 + CAP, :], banks[0][0:CAP, :], ACT.Silu).then_inc(G["ov_hs"], 1)
                    act.wait_ge(G["ov_turned"], j + 1)
                    act.activation(m.ht[:, :, 0:CAP],
                                   turned[:, :, 0:CAP], ACT.Copy)\
                       .then_inc(G["ov_ht"], 1)
                    act.wait_ge(G["ov_y"], j + 1)
                    act.dma_start(y_rows[bass.ds(2 * CAP * (j + MAIN), 2 * CAP), :], m.yo[0][0:64, :])\
                       .then_inc(G["ov_sent"], 16)
                    act.wait_ge(G["ov_sent"], 16 * j + 32)

        @block.vector
        def _(dve):
            dve.sem_inc(G["yo_ready"], 2)

            def picks(width, n0):
                io = m.iota[:, 0:width].unsqueeze(1).broadcast_to([P, T, width])
                for k, g in enumerate((m.G1, m.G)):
                    dve.tensor_tensor(g[:, :, 0:width], io,
                                      m.yrel[:, k, :].unsqueeze(2).broadcast_to([P, T, width]),
                                      ALU.is_equal).then_inc(G["g_step"], 1)
                dve.wait_ge(G["g_step"], n0 + 2)

            picks(P, 0)
            dve.tensor_tensor(m.G, m.G, m.G1, ALU.add).then_inc(G["g_ready"], 1)
            with dve.Fori(0, NIT) as i:
                dve.wait_ge(G["g_ready"], i + 1)
                dve.tensor_scalar(m.yrel, m.yrel, -float(P), None, ALU.add).then_inc(G["g_step"], 1)
                dve.wait_ge(G["g_step"], 3 * i + 3)
                dve.wait_ge(G["gather_done"], 2 * i + 2)
                picks(P, 3 * i + 3)
                dve.tensor_tensor(m.G, m.G, m.G1, ALU.add).then_inc(G["g_ready"], 1)
                for pr in range(2):
                    dve.wait_ge(G["hs_ready"], 2 * i + pr + 1)
                    dve.tensor_tensor(m.hid[0:64, :], banks[pr][64:128, :], m.hs[64:128, :], ALU.mult)\
                       .then_inc(G["hid_ready"], 1)
                    dve.wait_ge(G["down_done"], 2 * i + pr + 2)
                    dve.wait_ge(G[f"y_sent{pr}"], 16 * i + 16)
                    dve.tensor_copy(m.yo[pr], banks[3 + pr][:, :]).then_inc(G["yo_ready"], 1)
            n = dve.value_load(m.misc_i[0:1, 1:2], min_val=0, max_val=MORE - 1)
            with dve.If(n > 0):
                dve.wait_ge(G["gather_done"], 2 * NIT + 2)
                dve.wait_ge(G["g_ready"], NIT + 1)
                dve.wait_ge(G["g_step"], 3 * NIT + 2)
                dve.wait_ge(G["y_sent0"], 16 * NIT + 16)
                dve.sem_inc(G["ov_step"], 1)
                with dve.Fori(0, n) as j:
                    dve.wait_ge(G["ov_step"], j + 1)
                    picks(CAP, 3 * NIT + 2 + 2 * j)
                    dve.tensor_tensor(m.G[:, :, 0:CAP], m.G[:, :, 0:CAP], m.G1[:, :, 0:CAP], ALU.add)\
                       .then_inc(G["ov_g"], 1)
                    dve.tensor_scalar(m.yrel, m.yrel, -float(CAP), None, ALU.add).then_inc(G["ov_step"], 1)
                    dve.wait_ge(G["ov_hs"], j + 1)
                    dve.tensor_tensor(m.hid[0:CAP, :], banks[0][64:64 + CAP, :], m.hs[64:64 + CAP, :],
                                      ALU.mult).then_inc(G["ov_hid"], 1)
                    dve.wait_ge(G["ov_down"], j + 2)
                    dve.wait_ge(G["ov_sent"], 16 * j + 16)
                    dve.tensor_copy(m.yo[0][0:64, :], banks[3][0:64, :]).then_inc(G["ov_y"], 1)


def combine_block(nc, m, G, banks, y_slots):
    with nc.Block() as block:

        @block.gpsimd
        def _(pool):
            for n in range(16):
                k, half, t = n % 2, n // 2 % 2, n // 4
                pool.indirect_dma_start(
                    out=m.yg[n], out_offset=None, in_=y_slots,
                    in_offset=bass.IndirectOffsetOnAxis(ap=m.yidx_i[:, 2 * half + k, t:t + 1], axis=0))\
                    .then_inc(G[f"y_in{n}"], 16)

        @block.vector
        def _(dve):
            for n in range(16):
                k, half, t = n % 2, n // 2 % 2, n // 4
                dve.wait_ge(G[f"y_in{n}"], 16)
                if n:
                    dve.wait_ge(G["combined"], n)
                hs = m.h[:, t, 512 * half:512 * half + 512]
                dve.scalar_tensor_tensor(hs, m.yg[n], m.gate[:, k, t:t + 1], hs, ALU.mult, ALU.add)\
                   .then_inc(G["combined"], 1)


L2 = 2
QL, KL, RP = 384, 256, 64
MH, MN, MV = 4, 128, 128
PW = (2, 4, 8, 16)
XH, XD = 4, 64
DFF = 2816
NJ = DFF // P
ALPHA = (2 * L2) ** 0.25
LN_EPS = 1e-5
C_CQ, C_XP, C_XQ, C_XV, C_IF = 0, 704, 960, 1216, 1728
RAW = QL + KL + RP + 8
LSLOT = 3
SLOT = KT * 512


def layer_memory(arena):
    m = persistent(arena)
    sp = Space(arena, m.free)
    m.norm_at = sp.at
    n = Space(arena, m.norm_at)
    m.qnT, m.knT = n(MH, S), n(MH, S)
    m.raw = n(T, RAW)
    m.so = n(T, XH * XD)
    m.over_end = n.at
    sp.at = m.norm_at + 8300
    assert m.over_end <= sp.at
    m.trig_at = sp.at
    m.cos, m.sin, m.nsin = (sp(T, HD // 2) for _ in range(3))
    m.trig = Space(arena, m.trig_at)(3 * T * HD // 2)
    m.causal = sp(S)
    m.upto, m.ones = sp(P), sp(P)
    m.band = sp(12, P)
    m.sel = sp(MH, P)
    m.slots = [sp(SLOT) for _ in range(LSLOT)]
    m.wf = sp(NJ, 4)
    m.ff_at = sp.at
    m.wuq = m.slots[1][:, 0:3 * 768].rearrange("p (k n) -> p k n", k=3)
    m.wukv = m.slots[2][:, 0:2 * 1024].rearrange("p (k n) -> p k n", k=2)
    at = sp.at
    m.lT = sp(6, S)
    m.sdx = [Space(arena, at + 1280 * i)(1280) for i in range(2)]
    m.gain6 = sp(6)
    m.kra, m.krb, m.krr = sp(T, 2, 32), sp(T, 2, 32), sp(T, 2 * RP)
    m.vt = sp(T, MH * MV)
    m.ra = [sp(4, 2, 32) for _ in range(2)]
    m.rb = [sp(4, 2, 32) for _ in range(2)]
    m.rot = [sp(4 * RP) for _ in range(2)]
    m.qpT = sp(2, S)
    at = sp.at
    m.xp = Space(arena, at)(T, 256)
    m.ssb = [sp(S) for _ in range(2)]
    m.pt = sp(S)
    m.mx, m.negm, m.den, m.rden = ([sp(1) for _ in range(2)] for _ in range(4))
    m.ya = sp(T, MH * MV)
    m.wp, m.wmq, m.wmk = sp(2, 64), sp(2, 64), sp(2, 64)
    m.spool = sp(2)
    m.wc = sp(2, 5)
    at = sp.at
    m.xq = sp(2, 3 + S)
    m.cv = sp(2, S)
    m.hm, m.hm2 = (Space(arena, at + T * XH * XD * i)(T * XH, XD) for i in range(2))
    m.hmt = Space(arena, at)(T, XH * XD)
    m.cT = sp(2, S)
    m.mqT, m.mkT = sp(2, S), sp(2, S)
    m.vx = sp(T, XH, XD + 1)
    m.gb = sp(8)
    m.gmh = sp(XH * XD)
    m.g = [sp(T, XH) for _ in range(12)]
    m.cm = sp(S)
    at = sp.at
    m.yp = Space(arena, at)(2, S)
    m.wt = [sp(S) for _ in range(2)]
    m.st = [sp(T * XH) for _ in range(3)]
    m.ssq, m.rs2, m.rs1 = sp(2, T), sp(2, T), sp(2, T)
    m.nhalf2 = sp(1)
    m.mixT = m.aT
    f = Space(arena, m.ff_at)
    m.hidT = f(NJ, S)
    m.gp = [f(2 + S) for _ in range(2)]
    m.gconv = [f(S) for _ in range(2)]
    m.gs = [f(S) for _ in range(2)]
    return m




LAYER_COUNTS = {
    "l_small": 16 * 9, "lw_in0": 16 * 3, "lw_in1": 16 * 4, "lw_in2": 16 * 2, "l_proj": 34,
    "l_read": 30, "l_pre": 3, "l_latent_rs": 2, "l_latent": 2, "l_kr": 1, "l_turn": 8, "l_turned": 8,
    "l_rope": 4, "l_rot": 4, "l_qturn": 4, "l_qT": 4, "l_gate": 2, "l_gexp": 2, "l_logf": 1,
    "l_cum": 1, "l_a": 1, "l_arow": 1, "l_cm": 1, "l_cmT": 1, "l_pool": 2, "l_poolr": 2, "l_pw": 2,
    "l_pmix": 2, "l_conv": 2, "l_cT": 2, "l_mqk": 4, "l_mqkr": 4, "l_s": 16, "l_negm": 16,
    "l_exp": 16, "l_pt": 16, "l_ptr": 16, "l_pv": 16, "l_ya": 16, "l_cmb": 4, "l_ms": 16,
    "l_wd": 16, "l_we": 16, "l_wm": 16, "l_sd": 16, "l_pv2": 4, "l_hm": 4, "l_var": 1, "l_rs": 1,
    "l_sg": 1, "l_mout": 1, "l_ret": 8, "l_retr": 8, "l_out": 8, "l_res": 8,
    "f_in0": 16 * 10, "f_in1": 16 * 8, "f_in2": 16 * 10, "f_small": 16, "f_zero": 1, "f_g": 22, "f_a": 22, "f_gcopy": 22,
    "f_conv": 22, "f_silu": 22, "f_hid": 22, "f_down": 8, "f_out": 8, "f_down_k": 21,
}
STEPS2 = ["l_dve", "l_pl"]


class At:

    def __init__(self, G, eng, layer):
        self.G, self.eng, self.layer, self.seen = G, eng, layer, {}

    def __call__(self, name, n):
        if n > self.seen.get(name, 0):
            assert n <= LAYER_COUNTS[name], (name, n)
            self.eng.wait_ge(self.G[name], LAYER_COUNTS[name] * self.layer + n)
            self.seen[name] = n


class Own:

    def __init__(self, eng, sem, counts):
        self.eng, self.sem, self.counts = eng, sem, counts

    def __call__(self, ins):
        ins.then_inc(self.sem, 1)
        self.counts[self.sem.name] = self.counts.get(self.sem.name, 0) + 1
        return self.counts[self.sem.name]

    def wait(self, n):
        self.eng.wait_ge(self.sem, n)

    def do(self, ins):
        self.wait(self(ins))


def band_tables():
    r, c = np.arange(P)[:, None], np.arange(P)[None, :]
    out = []
    for w in PW:
        near = (r <= c) & (r > c - w)
        out.append(near / np.minimum(c + 1, w).astype(np.float32) - (r == c))
        out.append(near / np.float32(w) - (r == c))
        out.append((r - P > c - w) / np.float32(w))
    return np.concatenate(out, axis=1)


def later_constants():
    r, c = np.arange(P)[:, None], np.arange(S)[None, :]
    t = {"causal": np.where(c - WOFF <= r, 0.0, NEG), "upto": (r <= c[:, :P]) * 1.0, "ones2": np.ones((P, P)),
         "band": band_tables(), "sel": (r == c // P) * 1.0}
    return {k: np.ascontiguousarray(v, dtype=np.float32) for k, v in t.items()}


def log_sigmoid(own, dve, x, tmps, out, exp_in, exp_wait):
    neg, z, r, r2, s, lo = tmps
    own.do(dve.tensor_scalar(neg, x, -1.0, None, ALU.mult))
    own(dve.tensor_scalar(lo, x, 0.0, None, ALU.min))
    exp_in(dve.tensor_tensor(neg, neg, x, ALU.min))
    exp_wait()
    own.do(dve.tensor_scalar(r2, z, 2.0, None, ALU.add))
    own.do(dve.reciprocal(r2, r2))
    own.do(dve.tensor_tensor(r, z, r2, ALU.mult))
    own.do(dve.tensor_tensor(r2, r, r, ALU.mult))
    own.do(dve.tensor_scalar(s, r2, 1.0 / 19, 1.0 / 17, ALU.mult, ALU.add))
    for k in (15, 13, 11, 9, 7, 5, 3, 1):
        own.do(dve.tensor_tensor(s, s, r2, ALU.mult))
        own.do(dve.tensor_scalar(s, s, 1.0 / k, None, ALU.add))
    own.do(dve.tensor_tensor(s, s, r, ALU.mult))
    return dve.scalar_tensor_tensor(out, s, -2.0, lo, ALU.mult, ALU.add)


def sd_at(st):
    return sum(S - P * i for i in range(st))


def slot_view(m, i):
    return m.slots[i].rearrange("p (k n) -> p k n", k=KT)


def layer_mixer_block(nc, m, G, banks, A, l, own_counts):
    def g4(x):
        return x.rearrange("p (t h) d -> p t h d", t=T)

    def read_count(n):
        if 18 <= n < 22:
            return "l_rope", n - 17
        return "l_read", n + 1 if n < 18 else n - 3

    hrows = lambda h: slice(64 * (h % 2), 64 * (h % 2) + 64)

    with nc.Block() as block:

        @block.sync
        def _(sp):
            need = At(G, sp, l)
            w = A["w_in_2"][l].rearrange("(k p) n -> p k n", p=P)

            def load(name, dst, src):
                sp.dma_start(dst, src, allow_slow_non_contiguous=True).then_inc(G[name], 16)

            load("lw_in0", slot_view(m, 0)[:, :, 0:QL], w[:, :, 0:QL])
            load("lw_in1", slot_view(m, 1)[:, :, 0:KL + RP], w[:, :, QL:C_XP])
            load("lw_in1", slot_view(m, 1)[:, :, KL + RP:KL + RP + 8], w[:, :, C_IF:C_IF + 8])
            load("lw_in2", slot_view(m, 2), w[:, :, C_XP:C_XV])
            load("l_small", m.gain6[:, 0:5], A["gain_cols"][l])
            load("l_small", m.gb, A["gate_bias"][l].partition_broadcast(P))
            load("l_small", m.wc, A["mconv_cols"][l])
            load("l_small", m.spool, A["s_pool_cols"][l])
            load("l_small", m.gmh, A["g_mh_2"][l].partition_broadcast(P))
            for dst, name in ((m.wp, "w_pool_2"), (m.wmq, "w_mq_2"), (m.wmk, "w_mk_2")):
                load("l_small", dst, A[name][l].rearrange("(a b) c d -> (b c) a d", b=2))
            load("l_small", m.wf, A["fconv_cols"][l])
            need("l_proj", 4)
            load("lw_in0", slot_view(m, 0), w[:, :, C_XV:C_IF])
            need("l_proj", 8)
            load("lw_in1", m.wuq, A["w_uq_2"][l].rearrange("(k p) n -> p k n", p=P))
            need("l_proj", 14)
            load("lw_in2", m.wukv, A["w_ukv_2"][l].rearrange("(k p) n -> p k n", p=P))
            wo = A["w_out_2"][l].rearrange("(k p) n -> p k n", p=P)
            need("l_proj", 18)
            load("lw_in0", slot_view(m, 0), wo[:, :, 0:512])
            need("l_proj", 34)
            load("lw_in1", slot_view(m, 1), wo[:, :, 512:1024])

        @block.tensor
        def _(pe):
            need = At(G, pe, l)

            def group(n, terms, out, wait_for=()):
                for name, k in wait_for:
                    need(name, k)
                if n >= 2:
                    need(*read_count(n - 2))
                for i, (a, b) in enumerate(terms):
                    ins = pe.matmul(out, a, b, start=(i == 0), stop=(i == len(terms) - 1))
                ins.then_inc(G["l_proj"], 1)

            s0, s1, s2 = (slot_view(m, i) for i in range(3))
            ks = range(KT)
            for t in range(T):
                group(t, [(m.aT[:, k, tile(t)], s0[:, k, 0:QL]) for k in ks],
                      banks[t % 2][:, 0:QL], [("lw_in0", 16)])
            for t in range(T):
                group(4 + t, [(m.aT[:, k, tile(t)], s1[:, k, 0:328]) for k in ks],
                      banks[t % 2][:, 0:328], [("lw_in1", 32)])
            for t in range(T):
                group(8 + t, [(m.aT[:, k, tile(t)], s2[:, k, 0:256]) for k in ks],
                      banks[t % 2][:, 0:256], [("lw_in2", 16)])
            for j in range(2):
                group(12 + j, [(s2[:, k, 256 + P * j:256 + P * j + P], m.aT[:, k, :]) for k in ks],
                      banks[j][:, :])
            for t in range(T):
                group(14 + t, [(m.aT[:, k, tile(t)], s0[:, k, :]) for k in ks],
                      banks[t % 2][:, :], [("lw_in0", 32)])
            for x in range(2 * T):
                t, part = x // 2, x % 2
                need("l_latent", part + 1)
                if part:
                    need("l_kr", 1)
                need("l_turned", x - 1)
                for j in range(3):
                    src = m.krr[:, t, :] if part and j == 2 else m.raw[:, t, tile(3 * part + j)]
                    ins = pe.transpose(banks[2 + part][:, tile(j)], src, m.ident)
                ins.then_inc(G["l_turn"], 1)
            need("l_small", LAYER_COUNTS["l_small"])
            for pr in range(2):
                need("l_read", 12)
                for gg in range(2):
                    g, rows = 2 * pr + gg, slice(64 * gg, 64 * gg + 64)
                    for t in range(T):
                        pe_ins = pe.matmul(banks[6 + pr][rows, tile(t)], m.xp[:, t, 64 * g:64 * g + 64],
                                           m.band[:, 3 * g + (t > 0), :], start=True, stop=(t == 0))
                        if t:
                            pe_ins = pe.matmul(banks[6 + pr][rows, tile(t)], m.xp[:, t - 1, 64 * g:64 * g + 64],
                                               m.band[:, 3 * g + 2, :], start=False, stop=True)
                pe_ins.then_inc(G["l_pool"], 1)
            need("l_turned", 8)
            need("l_logf", 1)
            for t in range(T):
                for u in range(t + 1):
                    ins = pe.matmul(banks[2][:, XH * t:XH * t + XH], m.ones if u < t else m.upto,
                                    m.g[7][:, u, :], start=(u == 0), stop=(u == t))
            ins.then_inc(G["l_cum"], 1)
            for pr in range(2):
                need("l_poolr", pr + 1)
                for gg in range(2):
                    rows = slice(64 * gg, 64 * gg + 64)
                    ins = pe.matmul(banks[6 + pr][rows, :], m.wp[rows, pr, :], m.yp[rows, pr, :],
                                    start=True, stop=True)
                ins.then_inc(G["l_pw"], 1)
            wq = m.wuq.rearrange("p k (h c) -> p k h c", h=MH)
            wkv = m.wukv.rearrange("p k (h c) -> p k h c", h=MH)
            for t in range(T):
                group(18 + t, [(m.lT[:, k, tile(t)], wq[:, k, :, MN:]) for k in range(3)],
                      banks[t % 2][:, 0:256].rearrange("p (h c) -> p h c", h=MH), [("lw_in1", 48)])
            need("l_a", 1)
            for t in range(T):
                ins = pe.transpose(banks[3][0:XH, tile(t)], m.g[9][:, t, :], m.ident)
            ins.then_inc(G["l_arow"], 1)
            for t in range(T):
                group(22 + t, [(m.lT[:, 3 + k, tile(t)], wkv[:, k, :, MN:]) for k in range(2)],
                      banks[t % 2][:, :].rearrange("p (h c) -> p h c", h=MH), [("lw_in2", 32)])
            for t in range(T):
                need("l_rot", t + 1)
                need("l_qT", t - 1)
                for j in range(2):
                    ins = pe.transpose(banks[4 + t % 2][:, tile(j)], m.rot[t % 2][:, tile(j)], m.ident)
                ins.then_inc(G["l_qturn"], 1)
            for h in range(MH):
                group(26 + h, [(wkv[:, k, h, 0:MN], m.lT[:, 3 + k, :]) for k in range(2)],
                      banks[h % 2][:, :])
            need("l_cm", 1)
            for t in range(T):
                ins = pe.transpose(banks[2][:, 16 + XH * t:16 + XH * t + XH], m.cm[0:XH, tile(t)],
                                   m.ident[0:XH, 0:XH])
            ins.then_inc(G["l_cmT"], 1)
            for h in range(MH):
                group(30 + h, [(wq[:, k, h, 0:MN], m.lT[:, k, :]) for k in range(3)],
                      banks[h % 2][:, :])
            need("l_pmix", 2)
            for y in range(4):
                pr, wm = y // 2, (m.wmq, m.wmk)[y % 2]
                need("l_cT", pr + 1)
                need("l_mqkr", y - 1)
                for hh in range(2):
                    rows = slice(64 * hh, 64 * hh + 64)
                    ins = pe.matmul(banks[6 + y % 2][rows, :], wm[rows, pr, :], m.cT[rows, pr, :],
                                    start=True, stop=True)
                ins.then_inc(G["l_mqk"], 1)

            need("l_qT", 4)
            need("l_read", 30)
            need("l_mqkr", 4)
            for n in range(18):
                if n < 16:
                    h, t = n // 4, n % 4
                    need("l_negm", n - 1)
                    cs = slice(0, P * (t + 1))
                    pe.matmul(banks[4 + n % 2][:, cs], m.qnT[:, h, tile(t)], m.knT[:, h, cs],
                              start=True, stop=False)
                    pe.matmul(banks[4 + n % 2][:, cs], m.qpT[hrows(h), h // 2, tile(t)],
                              m.lT[hrows(h), 5, cs], start=False, stop=True).then_inc(G["l_s"], 1)
                    h, st = n // 4, n % 4
                    if st == 0:
                        need("l_wd", 4 * h)
                        pe.matmul(banks[3][:, :], m.sel[0:XH, h, :], m.cm[0:XH, :],
                                  start=True, stop=True).then_inc(G["l_cmb"], 1)
                    need("l_sd", n - 1)
                    pe.matmul(banks[n % 2][:, 0:S - P * st], m.mkT[hrows(h), h // 2, tile(st)],
                              m.mqT[hrows(h), h // 2, P * st:], start=True, stop=True)\
                      .then_inc(G["l_ms"], 1)
                if 1 <= n <= 16:
                    h, t = (n - 1) // 4, (n - 1) % 4
                    need("l_exp", n)
                    need("l_ptr", n - 1)
                    for k in range(t + 1):
                        ins = pe.transpose(banks[6][:, tile(k)], m.ssb[(n - 1) % 2][:, tile(k)], m.ident)
                    ins.then_inc(G["l_pt"], 1)
                    need("l_ptr", n)
                    need("l_ya", n - 1)
                    for k in range(t + 1):
                        ins = pe.matmul(banks[7][:, 0:MV], m.pt[:, tile(k)], m.vt[:, k, MV * h:MV * h + MV],
                                        start=(k == 0), stop=(k == t))
                    ins.then_inc(G["l_pv"], 1)
                if n % 4 == 1 and n >= 5:
                    h = n // 4 - 1
                    need("l_sd", 4 * h + 4)
                    need("l_gate", 2)
                    need("l_hm", h)
                    for t in range(T):
                        for st in range(t + 1):
                            c = sd_at(st) + P * (t - st)
                            ins = pe.matmul(banks[2][:, 65 * t:65 * t + 65], m.sdx[h % 2][:, c:c + P],
                                            m.vx[:, st, h, :], start=(st == 0), stop=(st == t))
                    ins.then_inc(G["l_pv2"], 1)
            for x in range(8):
                t = x % 4
                if x < 4:
                    need("l_ya", 16)
                    need("l_negm", 16)
                else:
                    need("l_mout", 1)
                need("l_retr", x - 1)
                for j in range(4 if x < 4 else 2):
                    src = m.ya[:, t, tile(j)] if x < 4 else m.hmt[:, t, tile(j)]
                    ins = pe.transpose(banks[4 + x % 2][:, tile(j)], src, m.ident)
                ins.then_inc(G["l_ret"], 1)

        @block.scalar
        def _(act):
            need = At(G, act, l)
            for n in range(18):
                bank = banks[n % 2]
                need("l_proj", n + 1)
                if n < 8:
                    t, i = n % 4, n // 4
                    c0, width, lat = ((0, QL, QL), (QL, 328, KL))[i]
                    act.activation(m.raw[:, t, c0:c0 + width], bank[:, 0:width], ACT.Copy)
                    need("l_read", n - 1)
                    act.activation(m.wt[n % 2][:, 0:lat], bank[:, 0:lat], ACT.Square,
                                   accum_out=m.ssq[:, i, t:t + 1]).then_inc(G["l_read"], 1)
                elif n < 12:
                    act.activation(m.xp[:, n - 8, :], bank[:, 0:256], ACT.Copy).then_inc(G["l_read"], 1)
                elif n < 14:
                    act.activation(m.xq[:, n - 12, 3:], bank[:, :], ACT.Copy).then_inc(G["l_read"], 1)
                else:
                    t = n - 14
                    act.activation(m.vx[:, t, :, 0:XD], bank[:, 0:256].rearrange("p (h d) -> p h d", h=XH),
                                   ACT.Copy)
                    act.activation(m.so[:, t, :], bank[:, 256:512], ACT.Sigmoid).then_inc(G["l_read"], 1)
            need("l_gate", 1)
            act.activation(m.g[1], m.g[0], ACT.Exp).then_inc(G["l_gexp"], 1)
            for pr in range(2):
                need("l_pool", pr + 1)
                act.activation(m.yp[:, pr, :], banks[6 + pr][:, :], ACT.Copy).then_inc(G["l_poolr"], 1)
            need("l_small", LAYER_COUNTS["l_small"])
            for pr in range(2):
                need("l_pw", pr + 1)
                act.activation(m.mixT[:, 4 + pr, :], banks[6 + pr][:, :], ACT.Copy,
                               scale=m.spool[:, pr:pr + 1]).then_inc(G["l_pmix"], 1)
            for n in range(22, 26):
                need("l_proj", n + 1)
                act.activation(m.vt[:, n - 22, :], banks[n % 2][:, :], ACT.Copy).then_inc(G["l_read"], 1)
            for t in range(T):
                need("l_qturn", t + 1)
                act.activation(m.qpT[:, :, tile(t)],
                               banks[4 + t % 2][:, 0:256].rearrange("p (a c) -> p a c", a=2), ACT.Copy)\
                   .then_inc(G["l_qT"], 1)
            for n in range(26, 34):
                need("l_proj", n + 1)
                dst = m.knT[:, n - 26, :] if n < 30 else m.qnT[:, n - 30, :]
                act.activation(dst, banks[n % 2][:, :], ACT.Copy).then_inc(G["l_read"], 1)
            for pr in range(2):
                need("l_conv", pr + 1)
                act.activation(m.cT[:, pr, :], m.cv[:, pr, :], ACT.Silu).then_inc(G["l_cT"], 1)
            for y in range(4):
                need("l_mqk", y + 1)
                act.activation((m.mqT, m.mkT)[y % 2][:, y // 2, :], banks[6 + y % 2][:, :], ACT.Copy,
                               scale=1.0 if y % 2 == 0 else XD ** -0.5).then_inc(G["l_mqkr"], 1)
            need("l_gate", 2)
            act.activation(m.g[11], m.g[10], ACT.Exp, scale=-1.0).then_inc(G["l_gexp"], 1)
            for n in range(17):
                if n >= 1:
                    t = (n - 1) % 4
                    need("l_pt", n)
                    need("l_pv", n - 1)
                    act.activation(m.pt[:, 0:P * (t + 1)], banks[6][:, 0:P * (t + 1)], ACT.Copy)\
                       .then_inc(G["l_ptr"], 1)
                if n < 16:
                    t = st = n % 4
                    x = m.ssb[n % 2][:, 0:P * (t + 1)]
                    need("l_negm", n + 1)
                    act.activation(x, x, ACT.Exp, scale=(MN + RP) ** -0.5, bias=m.negm[n % 2],
                                   accum_out=m.den[n % 2]).then_inc(G["l_exp"], 1)
                    need("l_wd", n + 1)
                    x = m.wt[n % 2][:, 0:S - P * st]
                    act.activation(x, x, ACT.Exp, scale=-1.0).then_inc(G["l_we"], 1)
            for x in range(8):
                t, k = x % 4, 4 if x < 4 else 2
                need("l_ret", x + 1)
                act.activation(m.mixT[:, 0:4, tile(t)] if x < 4 else m.mixT[:, 6:8, tile(t)],
                               banks[4 + x % 2][:, 0:P * k].rearrange("p (a c) -> p a c", a=k), ACT.Copy)\
                   .then_inc(G["l_retr"], 1)

        @block.gpsimd
        def _(pool):
            need = At(G, pool, l)
            own = Own(pool, G["l_pl"], own_counts)
            pool.memset(m.xq[:, :, 0:3], 0.0).then_inc(G["l_pre"], 1)
            pool.memset(m.vx[:, :, :, XD:XD + 1], 1.0).then_inc(G["l_pre"], 1)
            pool.memset(m.gain6[:, 5:6], 1.0).then_inc(G["l_pre"], 1)
            own.do(pool.memset(m.nhalf2, -0.5))
            for i, width in enumerate((QL, KL)):
                need("l_read", 4 * i + 4)
                own.do(pool.tensor_scalar(m.rs1[:, i, :], m.ssq[:, i, :], 1.0 / width, EPS, ALU.mult, ALU.add))
                pool.tensor_tensor(m.rs2[:, i, :], m.rs1[:, i, :], m.nhalf2.broadcast_to([P, T]), ALU.pow)\
                    .then_inc(G["l_latent_rs"], 1)
            need("l_read", 18)
            need("l_small", LAYER_COUNTS["l_small"])
            pool.tensor_tensor(m.so, m.so, m.gmh.unsqueeze(1).broadcast_to([P, T, XH * XD]), ALU.mult)\
                .then_inc(G["l_sg"], 1)
            for t in range(T):
                need("l_rope", t + 1)
                need("l_qturn", t - 1)
                pool.tensor_tensor(m.rot[t % 2], m.ra[t % 2].rearrange("p a b c -> p (a b c)"),
                                   m.rb[t % 2].rearrange("p a b c -> p (a b c)"), ALU.add)\
                    .then_inc(G["l_rot"], 1)
            for n in range(16):
                need("l_we", n + 1)
                x = m.wt[n % 2][:, 0:P]
                pool.tensor_tensor(x, x, m.upto, ALU.mult).then_inc(G["l_wm"], 1)
            need("l_var", 1)
            own.do(pool.tensor_scalar(m.st[2], m.st[1], 1.0 / XD, LN_EPS, ALU.mult, ALU.add))
            pool.tensor_tensor(m.st[2], m.st[2], m.nhalf2.broadcast_to([P, T * XH]), ALU.pow)\
                .then_inc(G["l_rs"], 1)

        @block.vector
        def _(dve):
            need = At(G, dve, l)
            own = Own(dve, G["l_dve"], own_counts)
            need("l_small", LAYER_COUNTS["l_small"])
            need("l_pre", 3)
            for i, (c0, width) in enumerate(((0, QL), (QL, KL))):
                need("l_latent_rs", i + 1)
                x = m.raw[:, :, c0:c0 + width]
                dve.tensor_tensor(x, x, m.rs2[:, i, :].unsqueeze(2).broadcast_to([P, T, width]), ALU.mult)\
                   .then_inc(G["l_latent"], 1)
            x = m.raw[:, :, QL + KL:QL + KL + RP].rearrange("p t (two d) -> p t two d", two=2)
            own(dve.tensor_tensor(m.kra, x, m.cos.unsqueeze(2).broadcast_to([P, T, 2, 32]), ALU.mult))
            own(dve.tensor_tensor(m.krb[:, :, 0, :], x[:, :, 1, :], m.nsin, ALU.mult))
            own.do(dve.tensor_tensor(m.krb[:, :, 1, :], x[:, :, 0, :], m.sin, ALU.mult))
            ka, kb = (z.rearrange("p t a b -> p t (a b)") for z in (m.kra, m.krb))
            dve.tensor_tensor(m.krr[:, :, 0:RP], ka, kb, ALU.add)
            dve.tensor_tensor(m.krr[:, :, RP:], ka, kb, ALU.add).then_inc(G["l_kr"], 1)
            gi, x = m.g[6], m.g[8]
            own(dve.tensor_tensor(gi, m.raw[:, :, 704:708], m.gb[:, 0:4].unsqueeze(1).broadcast_to([P, T, 4]), ALU.add))
            own.do(dve.tensor_tensor(x, m.raw[:, :, 708:712], m.gb[:, 4:8].unsqueeze(1).broadcast_to([P, T, 4]), ALU.add))
            log_sigmoid(own, dve, x, m.g[0:6], m.g[7], lambda ins: ins.then_inc(G["l_gate"], 1),
                        lambda: need("l_gexp", 1)).then_inc(G["l_logf"], 1)
            for x in range(2 * T):
                t, part = x // 2, x % 2
                need("l_turn", x + 1)
                dve.tensor_tensor(m.lT[:, 3 * part:3 * part + 3, tile(t)],
                                  banks[2 + part][:, 0:3 * P].rearrange("p (a c) -> p a c", a=3),
                                  m.gain6[:, 3 * part:3 * part + 3].unsqueeze(2).broadcast_to([P, 3, P]),
                                  ALU.mult).then_inc(G["l_turned"], 1)
            need("l_pre", 3)
            for j in range(2):
                need("l_read", 13 + j)
                own.do(dve.tensor_scalar(m.cv[:, j, :], m.xq[:, j, 0:S], m.wc[:, j, 0:1], m.wc[:, j, 4:5],
                                         ALU.mult, ALU.add))
                for k in range(1, 4):
                    ins = dve.scalar_tensor_tensor(m.cv[:, j, :], m.xq[:, j, k:k + S], m.wc[:, j, k:k + 1],
                                                   m.cv[:, j, :], ALU.mult, ALU.add)
                    if k < 3:
                        own.do(ins)
                ins.then_inc(G["l_conv"], 1)
            need("l_cum", 1)
            b, a = m.g[8], m.g[9]
            own.do(dve.tensor_copy(b, banks[2][:, 0:16].rearrange("p (t h) -> p t h", t=T)))
            dve.tensor_tensor(a, gi, b, ALU.subtract).then_inc(G["l_a"], 1)
            for t in range(T):
                n = 18 + t
                need("l_proj", n + 1)
                need("l_rot", t - 1)
                x = banks[n % 2][:, 0:256].rearrange("p (h two d) -> p h two d", h=4, two=2)
                cos = m.cos[:, t, :].unsqueeze(1).unsqueeze(1).broadcast_to([P, 4, 2, 32])
                sin = m.sin[:, t, :].unsqueeze(1).broadcast_to([P, 4, 32])
                nsin = m.nsin[:, t, :].unsqueeze(1).broadcast_to([P, 4, 32])
                dve.tensor_tensor(m.ra[t % 2], x, cos, ALU.mult)
                dve.tensor_tensor(m.rb[t % 2][:, :, 0, :], x[:, :, 1, :], nsin, ALU.mult)
                dve.tensor_tensor(m.rb[t % 2][:, :, 1, :], x[:, :, 0, :], sin, ALU.mult)\
                   .then_inc(G["l_rope"], 1)
            need("l_arow", 1)
            own.do(dve.tensor_copy(m.cm[0:XH, :], banks[3][0:XH, :]))
            dve.tensor_tensor_scan(m.cm[0:XH, :], m.cm[0:XH, :], m.cm[0:XH, :], 0.0, ALU.max, ALU.max)\
               .then_inc(G["l_cm"], 1)
            need("l_cmT", 1)
            dve.tensor_tensor(m.g[10], b, banks[2][:, 16:32].rearrange("p (t h) -> p t h", t=T), ALU.add)\
               .then_inc(G["l_gate"], 1)
            need("l_gexp", 2)
            em = m.g[11]
            need("l_pool", 2)
            need("l_pw", 2)
            need("l_cT", 2)
            for n in range(18):
                if n < 16:
                    h, t = n // 4, n % 4
                    w = P * (t + 1)
                    need("l_s", n + 1)
                    need("l_pt", n - 1)
                    c0 = WOFF - P * t
                    own.do(dve.tensor_tensor_reduce(
                        out=m.ssb[n % 2][:, 0:w], in0=banks[4 + n % 2][:, 0:w], in1=m.causal[:, c0:c0 + w],
                        scale=1.0, scalar=-3.0e38, op0=ALU.add, op1=ALU.max, accum_out=m.mx[n % 2]))
                    need("l_exp", n - 1)
                    dve.tensor_scalar(m.negm[n % 2], m.mx[n % 2], -(MN + RP) ** -0.5, None, ALU.mult)\
                       .then_inc(G["l_negm"], 1)
                    st = n % 4
                    need("l_cmb", h + 1)
                    need("l_sd", n - 1)
                    dve.tensor_scalar(m.wt[n % 2][:, 0:S - P * st], banks[3][:, P * st:],
                                      a[:, st, h:h + 1], 0.0, ALU.subtract, ALU.max)\
                       .then_inc(G["l_wd"], 1)
                if 1 <= n <= 16:
                    k = n - 1
                    h, st = k // 4, k % 4
                    w = S - P * st
                    need("l_wm", n)
                    need("l_ms", n)
                    need("l_pv2", h - 1)
                    dve.tensor_tensor(m.sdx[h % 2][:, sd_at(st):sd_at(st) + w], banks[k % 2][:, 0:w],
                                      m.wt[k % 2][:, 0:w], ALU.mult).then_inc(G["l_sd"], 1)
                    t = k % 4
                    need("l_exp", n)
                    c = own(dve.reciprocal(m.rden[k % 2], m.den[k % 2]))
                    need("l_pv", n)
                    own.wait(c)
                    dve.tensor_scalar(m.ya[:, t, MV * h:MV * h + MV], banks[7][:, 0:MV], m.rden[k % 2],
                                      None, ALU.mult).then_inc(G["l_ya"], 1)
                if n % 4 == 1 and n >= 5:
                    h = n // 4 - 1
                    need("l_pv2", h + 1)
                    x = banks[2][:, 0:65 * T].rearrange("p (t c) -> p t c", t=T)
                    d = m.g[0][:, :, h]
                    own.do(dve.scalar_tensor_tensor(d, x[:, :, XD], -1.0, em[:, :, h], ALU.mult, ALU.max))
                    own.do(dve.tensor_tensor(d, x[:, :, XD], d, ALU.max))
                    own.do(dve.reciprocal(d, d))
                    dve.tensor_tensor(g4(m.hm)[:, :, h, :], x[:, :, 0:XD], d.unsqueeze(2).broadcast_to([P, T, XD]),
                                      ALU.mult).then_inc(G["l_hm"], 1)
            dve.wait_ge(G["l_hm"], LAYER_COUNTS["l_hm"] * l + 4)
            n = T * XH
            wide = lambda x: x.unsqueeze(2).broadcast_to([P, n, XD])
            own.do(dve.tensor_reduce(m.st[0], m.hm, AX.X, ALU.add))
            own.do(dve.tensor_scalar(m.st[0], m.st[0], 1.0 / XD, None, ALU.mult))
            own.do(dve.tensor_tensor(m.hm, m.hm, wide(m.st[0]), ALU.subtract))
            own.do(dve.tensor_tensor(m.hm2, m.hm, m.hm, ALU.mult))
            dve.tensor_reduce(m.st[1], m.hm2, AX.X, ALU.add).then_inc(G["l_var"], 1)
            need("l_sg", 1)
            own.do(dve.tensor_tensor(m.hm, m.hm, m.so.rearrange("p t (h d) -> p (t h) d", h=XH), ALU.mult))
            need("l_rs", 1)
            dve.tensor_tensor(m.hm, m.hm, wide(m.st[2]), ALU.mult).then_inc(G["l_mout"], 1)


def ffn_loads(A, m, l):
    up = A["w_up_2"][l].rearrange("(k p) n -> p k n", p=P)
    down = A["w_down_2"][l].rearrange("(k p) n -> p k n", p=P)
    out = []
    for c in range(17):
        s = (c + 2) % 3
        if c < 11:
            v = slot_view(m, s)
            out.append([(v[:, :, 0:256], up[:, :, 256 * c:256 * c + 256]),
                        (v[:, :, 256:512], up[:, :, DFF + 256 * c:DFF + 256 * c + 256])])
        else:
            k = 4 * (c - 11)
            n = min(4, NJ - k)
            v = m.slots[s][:, 0:n * D].rearrange("p (k n) -> p k n", k=n)
            out.append([(v, down[:, k:k + n, :])])
    return out


def ffn_in(c):
    return 16 * sum(2 if i < 11 else 1 for i in range(c % 3, c + 1, 3))


def layer_out_block(nc, m, G, banks, A, l):
    with nc.Block() as block:

        @block.sync
        def _(sp):
            need = At(G, sp, l)
            loads = ffn_loads(A, m, l)
            for c in range(3):
                need("l_out", 4 * c)
                for dst, src in loads[c]:
                    sp.dma_start(dst, src).then_inc(G[f"f_in{(c + 2) % 3}"], 16)

        @block.tensor
        def _(pe):
            need = At(G, pe, l)
            need("l_retr", 8)
            for n in range(8):
                half, t = n // T, n % T
                need(f"lw_in{half}", LAYER_COUNTS[f"lw_in{half}"])
                for k in range(KT):
                    ins = pe.matmul(banks[n][:, :], m.mixT[:, k, tile(t)], slot_view(m, half)[:, k, :],
                                    start=(k == 0), stop=(k == KT - 1))
                ins.then_inc(G["l_out"], 1)

        @block.vector
        def _(dve):
            need = At(G, dve, l)
            for n in range(8):
                half, t = n // T, n % T
                need("l_out", n + 1)
                x = m.h[:, t, 512 * half:512 * half + 512]
                dve.scalar_tensor_tensor(x, x, ALPHA, banks[n][:, :], ALU.mult, ALU.add)\
                   .then_inc(G["l_res"], 1)


def ffn_block(nc, m, G, banks, A, l):
    def slot(c):
        return (c + 2) % 3

    with nc.Block() as block:

        @block.sync
        def _(sp):
            need = At(G, sp, l)
            loads = ffn_loads(A, m, l)
            for c in range(3, 17):
                p = c - 3
                if p < 11:
                    need("f_a", 2 * p + 2)
                else:
                    need("f_down_k", 4 * (p - 11) + 4)
                for dst, src in loads[c]:
                    sp.dma_start(dst, src).then_inc(G[f"f_in{slot(c)}"], 16)

        @block.tensor
        def _(pe):
            need = At(G, pe, l)
            for j in range(NJ):
                c = j // 2
                need(f"f_in{slot(c)}", ffn_in(c))
                w = slot_view(m, slot(c))
                for half, name, free in ((1, "f_g", "f_gcopy"), (0, "f_a", "f_hid")):
                    need(free, j - 1)
                    for k in range(KT):
                        c0 = 256 * half + P * (j % 2)
                        ins = pe.matmul(banks[2 * (j % 2) + half][:, :], w[:, k, c0:c0 + P], m.aT[:, k, :],
                                        start=(k == 0), stop=(k == KT - 1))
                    ins.then_inc(G[name], 1)
            for k in range(NJ):
                c = 11 + k // 4
                need(f"f_in{slot(c)}", ffn_in(c))
                need("f_hid", k + 1)
                v = m.slots[slot(c)].rearrange("p (k n) -> p k n", n=D)
                for t in (2, 3, 0, 1):
                    for half in range(2):
                        if k == 0 and t == 0:
                            need("f_hid", NJ)
                        ins = pe.matmul(banks[2 * t + half][:, :], m.hidT[:, k, tile(t)],
                                        v[:, k % 4, 512 * half:512 * half + 512],
                                        start=(k == 0), stop=(k == NJ - 1))
                        if k == NJ - 1:
                            ins.then_inc(G["f_down"], 1)
                if k < NJ - 1:
                    ins.then_inc(G["f_down_k"], 1)

        @block.scalar
        def _(act):
            need = At(G, act, l)
            for j in range(NJ + 1):
                if j < NJ:
                    need("f_g", j + 1)
                    need("f_conv", j - 1)
                    act.activation(m.gp[j % 2][:, 2:], banks[2 * (j % 2) + 1][:, :], ACT.Copy)\
                       .then_inc(G["f_gcopy"], 1)
                if j:
                    need("f_conv", j)
                    need("f_hid", j - 2)
                    act.activation(m.gs[(j - 1) % 2], m.gconv[(j - 1) % 2], ACT.Silu).then_inc(G["f_silu"], 1)

        @block.gpsimd
        def _(pool):
            for i in range(2):
                ins = pool.memset(m.gp[i][:, 0:2], 0.0)
            ins.then_inc(G["f_zero"], 1)

        @block.vector
        def _(dve):
            need = At(G, dve, l)
            own = Own(dve, G["l_dve"], G["own_counts"])
            need("f_zero", 1)
            for j in range(NJ + 1):
                if j < NJ:
                    gc, gp = m.gconv[j % 2], m.gp[j % 2]
                    need("f_gcopy", j + 1)
                    need("f_silu", j - 1)
                    own.do(dve.tensor_scalar(gc, gp[:, 0:S], m.wf[:, j, 0:1], m.wf[:, j, 3:4], ALU.mult, ALU.add))
                    own.do(dve.scalar_tensor_tensor(gc, gp[:, 1:1 + S], m.wf[:, j, 1:2], gc, ALU.mult, ALU.add))
                    dve.scalar_tensor_tensor(gc, gp[:, 2:2 + S], m.wf[:, j, 2:3], gc, ALU.mult, ALU.add)\
                       .then_inc(G["f_conv"], 1)
                if j:
                    i = j - 1
                    need("f_a", i + 1)
                    need("f_silu", i + 1)
                    dve.tensor_tensor(m.hidT[:, i, :], banks[2 * (i % 2)][:, :], m.gs[i % 2], ALU.mult)\
                       .then_inc(G["f_hid"], 1)
            for n, t, half in [(i, (2, 3, 0, 1)[i // 2], i % 2) for i in range(8)]:
                need("f_down", n + 1)
                x = m.h[:, t, 512 * half:512 * half + 512]
                dve.scalar_tensor_tensor(x, x, ALPHA, banks[2 * t + half][:, :], ALU.mult, ALU.add)\
                   .then_inc(G["f_out"], 1)


INPUTS = None


def program(nc, A, outs, stop=None, start=0):
    ctx = ExitStack()
    with ctx:
        arena = ctx.enter_context(nc.sbuf_tensor("arena", [P, ARENA], f32))
        banks = [ctx.enter_context(nc.psum_tensor(f"bank{i}", [P, 512], f32)) for i in range(8)]
        G = {n: ctx.enter_context(nc.semaphore(n)) for n in NORM_SEMS + ["x_in", "dbg", "later_in", "sent"]}
        G["norm_w_at"] = G["pool_at"] = G["dve_at"] = 0
        if start == 0:
            own = take(nc, G, MIXER_SEMS + MERGE_SEMS)
            m = mixer_memory(arena)
            norm_views(m, m.ring_at)
            load_x(nc, m, G, A)
            norm_block(nc, m, G, banks, 0, "rms", m.ns, A["norm_mix_w"][0])
            if stop == "n0":
                return dbg(nc, G, outs, m.aT)
            mixer_block(nc, m, G, banks, A)
            if stop == "mix":
                return dbg(nc, G, outs, m.y_att, m.y_ret)
            merge_block(nc, m, G, banks, A)
            if stop == "merge":
                return dbg(nc, G, outs, m.h)
            give_back(nc, G, own)
        if start <= 1:
            own = take(nc, G, ROUTER_SEMS + MOE_SEMS + COMB_SEMS)
            m = moe_memory(arena)
            norm_views(m, m.norm_at)
            if start == 1:
                load_x(nc, m, G, A)
            eb_dram = nc.dram_tensor("further_experts", (1, MORE), i32, kind="Internal").ap()
            y_slots = nc.dram_tensor("y_slots", ((MAIN + MORE) * 2 * CAP, 512), f32, kind="Internal").ap()
            norm_block(nc, m, G, banks, 1 - start, "rms", m.hn, A["norm_moe_w"][0])
            router_block(nc, m, G, banks, A, eb_dram, y_slots)
            moe_block(nc, m, G, banks, A, y_slots)
            combine_block(nc, m, G, banks, y_slots)
            if stop == "moe":
                return dbg(nc, G, outs, m.h)
            give_back(nc, G, own)
        m = layer_memory(arena)
        norm_views(m, m.norm_at)
        v = 2 - start
        for n in list(LAYER_COUNTS) + STEPS2:
            G[n] = ctx.enter_context(nc.semaphore(n))
        G["own_counts"] = {}
        if start == 2:
            load_x(nc, m, G, A)
        else:
            norm_block(nc, m, G, banks, v, "rms", m.h, A["norm_final_w"])
            v += 1
        later_block(nc, m, G, A)
        norm_block(nc, m, G, banks, v, "ln", m.h, A["ln0_g_2"], A["ln0_b_2"], LN_EPS, 0)
        for l in range(L2):
            layer_mixer_block(nc, m, G, banks, A, l, G["own_counts"])
            if stop == "mx":
                return dbg(nc, G, outs, m.mixT)
            layer_out_block(nc, m, G, banks, A, l)
            norm_block(nc, m, G, banks, v + 1 + 2 * l, "ln", m.h, A["ln1_g_2"][l], A["ln1_b_2"][l],
                       LN_EPS, 1 + 2 * l)
            if stop == "l1":
                return dbg(nc, G, outs, m.h, m.ya)
            ffn_block(nc, m, G, banks, A, l)
            norm_block(nc, m, G, banks, v + 2 + 2 * l, "ln", m.h, A["ln2_g_2"][l], A["ln2_b_2"][l],
                       LN_EPS, 2 + 2 * l)
            if stop == "l2":
                return dbg(nc, G, outs, m.h)
        with nc.Block() as block:

            @block.sync
            def _(sp):
                sp.dma_start(outs[0][0].rearrange("(t p) n -> p t n", p=P), m.h).then_inc(G["sent"], 16)
                sp.wait_ge(G["sent"], 16)


def take(nc, G, names):
    own = ExitStack()
    for n in names:
        G[n] = own.enter_context(nc.semaphore(n))
    return own, names


def give_back(nc, G, taken):
    own, names = taken
    with nc.Block() as block:

        @block.gpsimd
        def _(pool):
            for n in names:
                pool.sem_clear(G[n])

    own.close()


def load_x(nc, m, G, A):
    with nc.Block() as block:

        @block.sync
        def _(sp):
            sp.dma_start(m.h, A["x"][0].rearrange("(t p) n -> p t n", p=P)).then_inc(G["x_in"], 16)
            sp.dma_start(m.ident, A["consts"][:, 0:P]).then_inc(G["x_in"], 16)
            sp.wait_ge(G["x_in"], 32)


def later_block(nc, m, G, A):
    cols, _ = const_columns()
    at = {}
    n = 0
    for k, x in later_constants().items():
        at[k] = slice(n, n + x.shape[1])
        n += x.shape[1]
    with nc.Block() as block:

        @block.sync
        def _(sp):
            c2 = A["consts2"]
            c = cols["cos"][0]
            for dst, src in ((m.trig, A["consts"][:, c:c + 3 * T * HD // 2]), (m.causal, c2[:, at["causal"]]),
                             (m.upto, c2[:, at["upto"]]), (m.ones, c2[:, at["ones2"]]),
                             (m.band.rearrange("p a b -> p (a b)"), c2[:, at["band"]]),
                             (m.sel.rearrange("p a b -> p (a b)"), c2[:, at["sel"]])):
                sp.dma_start(dst, src).then_inc(G["later_in"], 16)
            sp.wait_ge(G["later_in"], 16 * 6)


def dbg(nc, G, outs, *views):
    with nc.Block() as block:

        @block.sync
        def _(sp):
            n = 0
            for o, v in zip(outs[1:], views):
                fl = v.rearrange("p a b -> p (a b)")
                sp.dma_start(o[:, 0:fl.shape[1]], fl).then_inc(G["dbg"], 16)
                n += 16
            sp.wait_ge(G["dbg"], n)


def host_layout(inputs):
    a = {k: np.ascontiguousarray(v) for k, v in inputs.items()}

    def cols(x):
        n, f = x.shape[1:]
        return np.ascontiguousarray(x.reshape(-1, n, f // P, P).transpose(0, 3, 2, 1))

    a["gain_cols"] = np.concatenate([cols(a["g_qn_2"][:, None])[..., 0], cols(a["g_kvn_2"][:, None])[..., 0]], 2)
    a["gate_bias"] = np.concatenate([a["b_i_2"], a["b_f_2"]], 1)
    a["mconv_cols"] = cols(np.concatenate([a["w_mconv_2"], a["b_mconv_2"][:, None]], 1))
    a["fconv_cols"] = cols(np.concatenate([a["w_fconv_2"], a["b_fconv_2"][:, None]], 1))
    a["s_pool_cols"] = cols(a["s_pool_2"][:, None])[..., 0]
    for k in ("g_qn_2", "g_kvn_2", "b_i_2", "b_f_2", "w_mconv_2", "b_mconv_2", "w_fconv_2", "b_fconv_2", "s_pool_2"):
        del a[k]
    a["consts"] = np.concatenate(list(constants().values()), axis=1)
    a["consts2"] = np.concatenate(list(later_constants().values()), axis=1)
    return a


def kernel(**inputs):
    import concourse.bacc as bacc
    from concourse.bass_utils import run_bass_kernel_spmd

    nc = bacc.Bacc("TRN2", target_bir_lowering=False, num_devices=1)
    a = host_layout(inputs)
    A = {k: nc.dram_tensor("in_" + k, v.shape, f32, kind="ExternalInput").ap() for k, v in a.items()}
    out = nc.dram_tensor("out", (1, S, D), f32, kind="ExternalOutput").ap()
    program(nc, A, [out])
    r = run_bass_kernel_spmd(nc, [{"in_" + k: v for k, v in a.items()}], core_ids=[0])
    return r.results[0]["out"]
```
